# Optimizing a Trainium2 kernel written in Bass

```python
import math
import jax, jax.numpy as jnp
from jax import lax
import numpy as np

D_MODEL = 1024
BATCH = 1
SEQ = 512
DEPTH = 1

SSD_HEADDIM = 64
SSD_HEADS = 24
SSD_INNER = SSD_HEADS * SSD_HEADDIM
SSD_GROUPS = 4
SSD_STATE = 128
SSD_CONV = 5
SSD_CHUNK = 128
SSD_BC = 2 * SSD_GROUPS * SSD_STATE
XBC_DIM = SSD_INNER + SSD_BC
S5_GROUP = 16
S5_WIDTH = 768
S5_GROUPS = S5_WIDTH // S5_GROUP
S5_STATE = 64
N_BRANCHES = 2
IN_COLS = SSD_INNER + XBC_DIM + 2 * SSD_HEADS + S5_WIDTH + N_BRANCHES * D_MODEL
SPLITS = (SSD_INNER, SSD_INNER + XBC_DIM, SSD_INNER + XBC_DIM + 2 * SSD_HEADS,
          SSD_INNER + XBC_DIM + 2 * SSD_HEADS + S5_WIDTH)
N_EXPERTS = 16
EXPERT_FF = 2816
CAPACITY_FACTOR = 2
DEEPNORM_ALPHA = (2.0 * DEPTH) ** 0.25
DEEPNORM_BETA = (8.0 * DEPTH) ** -0.25
LN_EPS = 1e-5
RMS_EPS = 1e-5
F32 = jnp.float32

kernel_name = "hybrid_ssd_s5_ec_moe_deepnorm"

def _layer_norm(x, g, b):
    xf = x.astype(F32)
    mu = jnp.mean(xf, -1, keepdims=True)
    var = jnp.mean(jnp.square(xf - mu), -1, keepdims=True)
    return ((xf - mu) * lax.rsqrt(var + LN_EPS) * g.astype(F32) + b.astype(F32)).astype(x.dtype)

def _dwconv_centred(x, w, b):
    k = w.shape[0]
    y = lax.conv_general_dilated(x, w[:, None, :].astype(x.dtype), window_strides=(1,),
                                 padding=[(k // 2, k // 2)],
                                 dimension_numbers=('NWC', 'WIO', 'NWC'),
                                 feature_group_count=x.shape[-1])
    return y + b.astype(x.dtype)

def _ssd_scan(xh, dt, a, bm, cm):
    bsz, l, h, p = xh.shape
    g, n = bm.shape[-2:]
    hg = h // g
    q = SSD_CHUNK
    c = l // q
    xdt = (xh.astype(F32) * dt[..., None]).reshape(bsz, c, q, g, hg, p)
    bc = bm.astype(F32).reshape(bsz, c, q, g, n)
    cc = cm.astype(F32).reshape(bsz, c, q, g, n)
    cs = jnp.cumsum((dt * a).reshape(bsz, c, q, g, hg), axis=2)
    seg = cs[:, :, :, None] - cs[:, :, None, :]
    mask = jnp.tril(jnp.ones((q, q), bool))[None, None, :, :, None, None]
    decay = jnp.where(mask, jnp.exp(jnp.where(mask, seg, 0.0)), 0.0)
    cb = jnp.einsum('bcqgn,bcsgn->bcqsg', cc, bc)
    wts = cb[..., None] * decay
    y_diag = jnp.einsum('bcqsgh,bcsghp->bcqghp', wts, xdt)
    last = cs[:, :, -1:]
    xw = xdt * jnp.exp(last - cs)[..., None]
    states = jnp.einsum('bcsgn,bcsghp->bcghpn', bc, xw)
    chunk_decay = jnp.exp(last[:, :, 0])

    def step(carry, inp):
        st, dec = inp
        return carry * dec[..., None, None] + st, carry

    init = jnp.zeros((bsz, g, hg, p, n), F32)
    _, prev = lax.scan(step, init, (jnp.moveaxis(states, 1, 0), jnp.moveaxis(chunk_decay, 1, 0)))
    prev = jnp.moveaxis(prev, 0, 1)
    y_off = jnp.einsum('bcqgn,bcghpn->bcqghp', cc, prev) * jnp.exp(cs)[..., None]
    return (y_diag + y_off).reshape(bsz, l, h, p)

def _ssd_branch(z, xbc, dt_raw, conv_w, conv_b, a_log_f, a_log_b, dt_bias_f, dt_bias_b,
                d_skip, norm_g, w_out):
    bsz, l, _ = z.shape
    xbc = jax.nn.silu(_dwconv_centred(xbc, conv_w, conv_b))
    xs, bm, cm = jnp.split(xbc, [SSD_INNER, SSD_INNER + SSD_BC // 2], axis=-1)
    xh = xs.reshape(bsz, l, SSD_HEADS, SSD_HEADDIM)
    bm = bm.reshape(bsz, l, SSD_GROUPS, SSD_STATE)
    cm = cm.reshape(bsz, l, SSD_GROUPS, SSD_STATE)
    dt_f_raw, dt_b_raw = jnp.split(dt_raw.astype(F32), 2, axis=-1)
    dt_f = jax.nn.softplus(dt_f_raw + dt_bias_f.astype(F32))
    dt_b = jax.nn.softplus(dt_b_raw + dt_bias_b.astype(F32))
    a_f = -jnp.exp(a_log_f.astype(F32))
    a_b = -jnp.exp(a_log_b.astype(F32))
    flip = lambda t: jnp.flip(t, axis=1)
    y_f = _ssd_scan(xh, dt_f, a_f, bm, cm)
    y_b = flip(_ssd_scan(flip(xh), flip(dt_b), a_b, flip(bm), flip(cm)))
    y = y_f + y_b + xh.astype(F32) * d_skip.astype(F32)[:, None]
    y = y.reshape(bsz, l, SSD_INNER) * jax.nn.silu(z.astype(F32))
    y = y.reshape(bsz, l, SSD_GROUPS, SSD_INNER // SSD_GROUPS)
    y = y * lax.rsqrt(jnp.mean(y * y, -1, keepdims=True) + RMS_EPS)
    y = y.reshape(bsz, l, SSD_INNER) * norm_g.astype(F32)
    return y.astype(z.dtype) @ w_out

def _s5_direction(ug, a_re, a_im, log_step, b_re, b_im):
    lam = lax.complex(a_re.astype(F32), a_im.astype(F32))
    step = jnp.exp(log_step.astype(F32))[:, None]
    a_bar = jnp.exp(lam * step)
    b_bar = ((a_bar - 1.0) / lam)[..., None] * lax.complex(b_re.astype(F32), b_im.astype(F32))
    bu = jnp.einsum('blgk,gpk->blgp', ug.astype(F32).astype(jnp.complex64), b_bar)
    a_seq = jnp.broadcast_to(a_bar, (1, ug.shape[1]) + a_bar.shape)

    def combine(e1, e2):
        a1, b1 = e1
        a2, b2 = e2
        return a2 * a1, a2 * b1 + b2

    _, states = lax.associative_scan(combine, (a_seq, bu), axis=1)
    return states

def _s5_branch(u, a_re_f, a_im_f, log_step_f, a_re_b, a_im_b, log_step_b,
               b_re, b_im, c_re, c_im, d_skip, w_glu_a, w_glu_b):
    bsz, l, _ = u.shape
    ug = u.reshape(bsz, l, S5_GROUPS, S5_GROUP)
    s_f = _s5_direction(ug, a_re_f, a_im_f, log_step_f, b_re, b_im)
    s_b = jnp.flip(_s5_direction(jnp.flip(ug, 1), a_re_b, a_im_b, log_step_b, b_re, b_im), 1)
    c = lax.complex(c_re.astype(F32), c_im.astype(F32))
    y = jnp.real(jnp.einsum('blgp,gkp->blgk', s_f + s_b, c)).reshape(bsz, l, S5_WIDTH)
    y = y + u.astype(F32) * d_skip.astype(F32)
    y = jax.nn.gelu(y).astype(u.dtype)
    return (y @ w_glu_a) * jax.nn.sigmoid(y @ w_glu_b)

def _expert_choice_ffn(x, w_router, w_e1, w_e3, w_e2):
    bsz, n, d = x.shape
    cap = CAPACITY_FACTOR * n // N_EXPERTS
    aff = jax.nn.softmax((x @ w_router).astype(F32), axis=-1)
    gate, idx = lax.top_k(jnp.swapaxes(aff, 1, 2), cap)
    xin = jax.vmap(lambda xb, ib: xb[ib])(x, idx)
    hid = jax.nn.silu(jnp.einsum('becd,edf->becf', xin, w_e1)) * jnp.einsum('becd,edf->becf', xin, w_e3)
    y = jnp.einsum('becf,efd->becd', hid, w_e2) * gate[..., None].astype(x.dtype)
    flat_idx = (idx + (jnp.arange(bsz, dtype=idx.dtype) * n)[:, None, None]).reshape(-1)
    out = jax.ops.segment_sum(y.reshape(-1, d), flat_idx, num_segments=bsz * n)
    return out.reshape(bsz, n, d)

def _layer(h, w_in, conv_w, conv_b, ssd_a_log_f, ssd_a_log_b, ssd_dt_bias_f, ssd_dt_bias_b,
           ssd_d, ssd_norm_g, w_out_ssd, s5_a_re_f, s5_a_im_f, s5_log_step_f, s5_a_re_b,
           s5_a_im_b, s5_log_step_b, s5_b_re, s5_b_im, s5_c_re, s5_c_im, s5_d, w_glu_a, w_glu_b,
           w_o, ln1_g, ln1_b, w_router, w_e1, w_e3, w_e2, ln2_g, ln2_b):
    proj = h @ w_in
    z, xbc, dt_raw, u, gates = jnp.split(proj, SPLITS, axis=-1)
    y_a = _ssd_branch(z, xbc, dt_raw, conv_w, conv_b, ssd_a_log_f, ssd_a_log_b,
                      ssd_dt_bias_f, ssd_dt_bias_b, ssd_d, ssd_norm_g, w_out_ssd)
    y_b = _s5_branch(u, s5_a_re_f, s5_a_im_f, s5_log_step_f, s5_a_re_b, s5_a_im_b, s5_log_step_b,
                     s5_b_re, s5_b_im, s5_c_re, s5_c_im, s5_d, w_glu_a, w_glu_b)
    g_a, g_b = jnp.split(gates, 2, axis=-1)
    mix = jax.nn.sigmoid(g_a) * y_a + jax.nn.sigmoid(g_b) * y_b
    h = _layer_norm(DEEPNORM_ALPHA * h + mix @ w_o, ln1_g, ln1_b)
    h = _layer_norm(DEEPNORM_ALPHA * h + _expert_choice_ffn(h, w_router, w_e1, w_e3, w_e2), ln2_g, ln2_b)
    return h

def setup_inputs(seed: int = 0) -> dict:
    key = jax.random.key(seed)
    ks = iter(jax.random.split(key, 48))
    L_ = DEPTH

    def nrm(shape, scale):
        return jax.random.normal(next(ks), (L_,) + shape, F32) * scale

    def unif(shape, lo, hi):
        return jax.random.uniform(next(ks), (L_,) + shape, F32, lo, hi)

    def dt_bias():
        dt = jnp.exp(unif((SSD_HEADS,), math.log(1e-3), math.log(1e-1)))
        return dt + jnp.log(-jnp.expm1(-dt))

    a_im_base = jnp.pi * jnp.arange(S5_STATE, dtype=F32)
    inp = {}
    inp["x"] = jax.random.normal(next(ks), (BATCH, SEQ, D_MODEL), F32)
    inp["w_in"] = nrm((D_MODEL, IN_COLS), D_MODEL ** -0.5)
    inp["conv_w"] = nrm((SSD_CONV, XBC_DIM), SSD_CONV ** -0.5)
    inp["conv_b"] = nrm((XBC_DIM,), 0.01)
    inp["ssd_a_log_f"] = jnp.log(unif((SSD_HEADS,), 1.0, 16.0))
    inp["ssd_a_log_b"] = jnp.log(unif((SSD_HEADS,), 1.0, 16.0))
    inp["ssd_dt_bias_f"] = dt_bias()
    inp["ssd_dt_bias_b"] = dt_bias()
    inp["ssd_d"] = 1.0 + nrm((SSD_HEADS,), 0.1)
    inp["ssd_norm_g"] = 1.0 + nrm((SSD_INNER,), 0.02)
    inp["w_out_ssd"] = nrm((SSD_INNER, D_MODEL), SSD_INNER ** -0.5)
    inp["s5_a_re_f"] = -0.5 + nrm((S5_GROUPS, S5_STATE), 0.01)
    inp["s5_a_im_f"] = a_im_base + nrm((S5_GROUPS, S5_STATE), 0.01)
    inp["s5_log_step_f"] = unif((S5_GROUPS,), math.log(1e-3), math.log(1e-1))
    inp["s5_a_re_b"] = -0.5 + nrm((S5_GROUPS, S5_STATE), 0.01)
    inp["s5_a_im_b"] = a_im_base + nrm((S5_GROUPS, S5_STATE), 0.01)
    inp["s5_log_step_b"] = unif((S5_GROUPS,), math.log(1e-3), math.log(1e-1))
    inp["s5_b_re"] = nrm((S5_GROUPS, S5_STATE, S5_GROUP), (2 * S5_GROUP) ** -0.5)
    inp["s5_b_im"] = nrm((S5_GROUPS, S5_STATE, S5_GROUP), (2 * S5_GROUP) ** -0.5)
    inp["s5_c_re"] = nrm((S5_GROUPS, S5_GROUP, S5_STATE), S5_STATE ** -0.5)
    inp["s5_c_im"] = nrm((S5_GROUPS, S5_GROUP, S5_STATE), S5_STATE ** -0.5)
    inp["s5_d"] = nrm((S5_WIDTH,), 1.0)
    inp["w_glu_a"] = nrm((S5_WIDTH, D_MODEL), S5_WIDTH ** -0.5)
    inp["w_glu_b"] = nrm((S5_WIDTH, D_MODEL), S5_WIDTH ** -0.5)
    inp["w_o"] = nrm((D_MODEL, D_MODEL), DEEPNORM_BETA * D_MODEL ** -0.5)
    inp["ln1_g"] = 1.0 + nrm((D_MODEL,), 0.02)
    inp["ln1_b"] = nrm((D_MODEL,), 0.02)
    inp["w_router"] = nrm((D_MODEL, N_EXPERTS), D_MODEL ** -0.5)
    inp["w_e1"] = nrm((N_EXPERTS, D_MODEL, EXPERT_FF), D_MODEL ** -0.5)
    inp["w_e3"] = nrm((N_EXPERTS, D_MODEL, EXPERT_FF), D_MODEL ** -0.5)
    inp["w_e2"] = nrm((N_EXPERTS, EXPERT_FF, D_MODEL), DEEPNORM_BETA * EXPERT_FF ** -0.5)
    inp["ln2_g"] = 1.0 + nrm((D_MODEL,), 0.02)
    inp["ln2_b"] = nrm((D_MODEL,), 0.02)
    return inp

def reference(x, w_in, conv_w, conv_b, ssd_a_log_f, ssd_a_log_b, ssd_dt_bias_f, ssd_dt_bias_b,
              ssd_d, ssd_norm_g, w_out_ssd, s5_a_re_f, s5_a_im_f, s5_log_step_f, s5_a_re_b,
              s5_a_im_b, s5_log_step_b, s5_b_re, s5_b_im, s5_c_re, s5_c_im, s5_d, w_glu_a, w_glu_b,
              w_o, ln1_g, ln1_b, w_router, w_e1, w_e3, w_e2, ln2_g, ln2_b):
    h = x
    for i in range(DEPTH):
        h = _layer(h, w_in[i], conv_w[i], conv_b[i], ssd_a_log_f[i], ssd_a_log_b[i],
                   ssd_dt_bias_f[i], ssd_dt_bias_b[i], ssd_d[i], ssd_norm_g[i], w_out_ssd[i],
                   s5_a_re_f[i], s5_a_im_f[i], s5_log_step_f[i], s5_a_re_b[i], s5_a_im_b[i],
                   s5_log_step_b[i], s5_b_re[i], s5_b_im[i], s5_c_re[i], s5_c_im[i], s5_d[i],
                   w_glu_a[i], w_glu_b[i], w_o[i], ln1_g[i], ln1_b[i], w_router[i], w_e1[i],
                   w_e3[i], w_e2[i], ln2_g[i], ln2_b[i])
    return h


_drawn_inputs = setup_inputs


def setup_inputs(seed=0):
    import zlib

    import numpy as np

    out = dict(_drawn_inputs(seed))
    spreads = {}
    factors = {'conv_b': 8.0,
     'ssd_d': 3.826,
     'ssd_norm_g': 21.216,
     's5_a_re_f': 64.0,
     's5_a_im_f': 49.064,
     's5_log_step_f': 46.264,
     's5_a_re_b': 64.0,
     's5_a_im_b': 47.632,
     's5_log_step_b': 46.096,
     's5_b_re': 46.56,
     's5_b_im': 46.424,
     's5_c_re': 47.352,
     's5_c_im': 46.072,
     'ln1_b': 2.742,
     'ln2_g': 24.356,
     'ln2_b': 23.056,
     'w_glu_b': 18.232,
     's5_d': 2.925,
     'w_glu_a': 2.694}
    for name, (base, spread) in spreads.items():
        noise = np.random.default_rng([zlib.crc32(name.encode()), seed]).standard_normal(out[name].shape)
        drawn = base * np.exp(spread * noise) if base else spread * noise
        out[name] = __import__('jax').numpy.asarray(drawn.astype(out[name].dtype))
    for name, factor in factors.items():
        out[name] = (out[name] * factor).astype(out[name].dtype)
    return out
```

```python
from contextlib import ExitStack

import numpy as np
import concourse.bass as bass
from concourse import mybir

F32 = mybir.dt.float32
ALU = mybir.AluOpType
ACT = mybir.ActivationFunctionType
AX = mybir.AxisListType

P = 128
D_MODEL, SEQ = 1024, 512
KT = D_MODEL // P
TT = SEQ // P
HEADS, HEADDIM, GROUPS = 24, 64, 4
HG = HEADS // GROUPS
GI = HG * HEADDIM
INNER = HEADS * HEADDIM
XBC = INNER + 2 * GROUPS * P
CONV = 5
S5_W, S5_K, S5_P = 768, 16, 64
S5_G = S5_W // S5_K
GP = S5_G // 2
T = 4
NC = SEQ // T
PARAMS = 24
QB = 4
NQ = GP // QB
COL_Z, COL_XBC = 0, INNER
COL_DT = COL_XBC + XBC
COL_U = COL_DT + 2 * HEADS
COL_GA = COL_U + S5_W
COL_GB = COL_GA + D_MODEL
EXPERTS, FF = 16, 2816
CAP = 2 * SEQ // EXPERTS
FC = 256
NCH = FF // FC
ALPHA = 2.0 ** 0.25
EPS = 1e-5

TWO_PI = 2 * np.pi
PI_1 = 6.28125
PI_2 = float(np.float32(np.floor((TWO_PI - PI_1) * 2 ** 22) / 2 ** 22))
PI_3 = float(np.float32(TWO_PI - PI_1 - PI_2))
ROUND = 12582912.0
PI_LIM = 3.1415925


class Space:

    def __init__(self, arena, at, end):
        self.arena, self.at, self.end = arena, at, end

    def take(self, *shape, parts=P):
        n = int(np.prod(shape))
        v = self.arena[0:parts, self.at:self.at + n]
        self.at += n
        assert self.at <= self.end, (self.at, self.end)
        if len(shape) > 1:
            names = "abcdef"[:len(shape)]
            v = v.rearrange(f"p ({' '.join(names)}) -> p {' '.join(names)}", **dict(zip(names, shape)))
        return v


class Steps:

    def __init__(self, eng, sem):
        self.eng, self.sem, self.n = eng, sem, 0

    def done(self, ins):
        ins.then_inc(self.sem, 1)
        self.n += 1
        return ins

    def wait(self):
        self.eng.wait_ge(self.sem, self.n)

    def link(self, ins):
        self.done(ins)
        self.wait()


def last(ap, n):
    s = list(ap.shape)
    return ap.unsqueeze(len(s)).to_broadcast(s + [n])


def mid2(ap, n):
    return ap.unsqueeze(2).to_broadcast([ap.shape[0], ap.shape[1], n, ap.shape[2]])


def first(ap, n):
    return ap.unsqueeze(1).to_broadcast([ap.shape[0], n, ap.shape[1]])


def weight_slices():
    s = [("w_in", 0, KT, COL_U, 512), ("w_in", 0, KT, COL_U + 512, 256), ("w_in", 0, KT, COL_DT, 2 * HEADS)]
    s += [("w_in", 0, KT, COL_XBC + 512 * i, 512) for i in range(XBC // 512)]
    s += [("w_in", 0, KT, COL_Z + GI * g, GI) for g in range(GROUPS)]
    for n in range(2):
        s += [("w_in", 0, KT, COL_GA + 512 * n, 512), ("w_out", 0, 6, 512 * n, 512), ("w_out", 6, 6, 512 * n, 512),
              ("w_in", 0, KT, COL_GB + 512 * n, 512), ("glu_b", 0, 6, 512 * n, 512), ("glu_a", 0, 6, 512 * n, 512)]
    s += [("w_o", 0, KT, 0, 512), ("w_o", 0, KT, 512, 512)]
    return s


def encoder(nc, A, out):
    SL = weight_slices()
    FIRST_Z = 3 + XBC // 512
    FIRST_MIX = FIRST_Z + GROUPS
    FIRST_WO = FIRST_MIX + 12
    NW = 2
    w_dram = {"w_in": A["w_in"][0], "w_out": A["w_out_ssd"][0], "glu_a": A["w_glu_a"][0],
              "glu_b": A["w_glu_b"][0], "w_o": A["w_o"][0]}
    u_dram = nc.dram_tensor("u_scratch", (S5_W, T, NC), F32, kind="Internal").ap()
    y_dram = nc.dram_tensor("y_scratch", (S5_W, T, NC), F32, kind="Internal").ap()
    toep_dram = nc.dram_tensor("toeplitz_scratch", (S5_W, (2 * T - 1) * S5_K), F32, kind="Internal").ap()

    with ExitStack() as ctx:
        WORDS = 53200
        arena = ctx.enter_context(nc.sbuf_tensor("arena", [P, WORDS], F32))
        ps = ctx.enter_context(nc.psum_tensor("ps", [P, 8, 512], F32))

        def sem(name):
            return ctx.enter_context(nc.semaphore(name))

        C = Space(arena, 0, 2300)
        ident, m_le, m_gt, m_ge, m_lt, ones = (C.take(P) for _ in range(6))
        chunk_no = C.take(NC)
        slot_no = C.take(CAP)
        eps_col = C.take(1)
        conv_w, conv_b = C.take(XBC // P, CONV), C.take(XBC // P)
        dt_bias, a_neg = C.take(2 * HEADS), C.take(2 * HEADS)
        d_row, norm_g = C.take(HEADS), C.take(INNER // P)
        dtime = C.take(TT, 2 * HEADS)
        da, w_end, e_cs, e_all = (C.take(TT, 2 * HEADS) for _ in range(4))
        C0 = C.at

        R = Space(arena, C0, WORDS)
        xT = R.take(KT, SEQ)
        ysT = R.take(S5_W // P, SEQ)
        wring = R.take(NW, KT, 512)
        yT_at = R.at
        uT = ysT
        S = Space(arena, R.at, WORDS)
        x_nat = S.take(TT, D_MODEL)
        vbd = x_nat.rearrange("p a b -> p (a b)").rearrange("p (n g d r c) -> p n g d r c", n=2, g=QB, d=2, r=2)
        U = S.take(GP, NC)
        M = S.take(GP, P)
        vc = S.take(2, QB, 2, 2, (T + 1) * S5_K)
        wc = S.take(QB, 2, 2, T * S5_K)
        wbd = S.take(QB, 2, 2, P)
        wT = S.take(2, 4, P)
        ty5 = U.rearrange("p g c -> p (g c)").rearrange("p (n w) -> p n w", n=S5_W // P)
        bbar = S.take(2, 2, GP, S5_K)
        c_map = S.take(2, GP, S5_K)
        bpad = S.take(QB, 2, 2, 2 * S5_K)
        par = S.take(2, 3, GP)
        small = S.take(32, 2, GP)
        pt = S.take(2, 2, 2, GP, T + 1)
        toep = S.take(2, QB, 2 * T - 1, S5_K, parts=2 * S5_K)
        eye2, d_diag, d_col = S.take(S5_K, parts=32), S.take(GP, S5_K, parts=32), S.take(GP, parts=32)
        tph, thf = S.take(QB * NC), S.take(QB * NC)
        cos_t, sin_t, decay = S.take(2, QB, NC), S.take(2, QB, NC), S.take(QB, NC)
        zr, zi, t1, t2, sr, si = (S.take(QB, NC) for _ in range(6))
        trd, trn = (x.rearrange("p g c -> p (g c)") for x in (zr, zi))
        E = Space(arena, S.at, WORDS)
        b_raw, c_nat = E.take(2, GP, S5_K), E.take(GP // 8, 2, P)
        par_raw = E.take(6, P, parts=GP)
        ls_raw = E.take(2, 2, parts=GP)
        vec_a, vec_b, vec_d = E.take(P, parts=120), E.take(P, parts=INNER // P), E.take(2 * S5_K, parts=GP)
        X = S.take(2, 2, 2, QB, NC)
        y5 = S.take(2, QB * NC)

        S = Space(arena, yT_at, WORDS)
        yT = S.take(INNER // P, SEQ)
        mix_at = S.at
        xs = S.take(TT, INNER)
        bn = S.take(TT, GROUPS * P)
        bT, cT = S.take(GROUPS, SEQ), S.take(GROUPS, SEQ)
        zg = S.take(2, TT, GI)
        st = S.take(2, TT, GI)
        xw = S.take(2, GI)
        ty = S.take(5, GI)
        rms = S.take(2, 4)
        S2 = Space(arena, S.at, WORDS)
        xraw = S2.take(4, SEQ + CONV - 1)
        cacc = S2.take(4, SEQ)
        xc = S2.take(4, SEQ)
        S = Space(arena, S.at, WORDS)
        rhs_f, rhs_b, dmat = S.take(HG, P), S.take(HG, P), S.take(HG, P)
        uf, emat, gmat = S.take(HG, P), S.take(HG, P), S.take(HG, P)

        S = Space(arena, mix_at, WORDS)
        sg_a, sg_b, sg_u = S.take(TT, 512), S.take(TT, 512), S.take(TT, 512)
        tmix = S.take(512)
        mix = S.take(TT, D_MODEL)
        mixT = S.take(2, KT, P)
        mix_end = S.at
        RING = 12 * 2048
        S = Space(arena, max(S.at, C0 + RING), WORDS)
        x_res = S.take(TT, D_MODEL)
        h = S.take(TT, D_MODEL)
        lnrow = S.take(2, D_MODEL)
        stats, mv = S.take(2, 6), S.take(8)
        acc = x_res
        S3 = Space(arena, C0, C0 + RING)
        hT = S3.take(KT, SEQ)
        w_r = S3.take(KT, EXPERTS)
        logit, ex_t = S3.take(TT, EXPERTS), S3.take(TT, EXPERTS)
        sm = S3.take(4, TT)
        affT, work, cum = (S3.take(SEQ, parts=EXPERTS) for _ in range(3))
        top8 = S3.take(CAP // 8, 8, parts=EXPERTS)
        ring = arena[:, C0:C0 + RING].rearrange("p (k n w) -> p k n w", k=6, n=2)
        S = Space(arena, C0 + RING, mix_end)
        aff, slotv = S.take(TT, EXPERTS), S.take(TT, EXPERTS)
        sel, selg = S.take(TT, 2, CAP), S.take(TT, 2, CAP)
        selgT = S.take(TT, P)
        xin = S.take(KT, P)
        s_h1, hid, hidT = S.take(2, 256), S.take(2, 256), S.take(2, 2, P)
        ye = S.take(D_MODEL)
        lnout, lnout2 = S.take(D_MODEL), S.take(D_MODEL)

        names = """x_loaded params_loaded broadcasts_loaded consts_ready consts_step xT_ps xT_copied vec_ps u_ps u_copied
        u_stored u_loaded dt_ps dt_added dt_abs dt_exp dt_ln da_ready seg_ps seg_exp seg_read wend_ready ls_filled
        step_exp lr_ready tanh_done theta_ready sin_done vw_ready bd_ready toep_ps toep_built toep_stored toep_loaded
        wT_ps wT_copied F_ps F_read angle_ready par_ready conv_tap sel_built tab_sin X_ready y5_ps y5_copied y5_stored y5_all yT5_loaded ysT_ready
        slice_used dve_step act_step pool_step m_cleared
        xbc_ps xbc_raw conv_done silu_done nat_ps nat_copied bn_copied
        z_ps z_silu xw_ready st_ps carried cb_ps segm_ps segm_exp mats_ready g_ready g_used yd_ps y_read gate_ready rms_sqrt yn_ready yt_ps yt_copied
        mix_ps mix_sig mix_read mix_ready mixT_ps mixT_copied wo_ps wo_read var_ready std_ready h_ready xres_loaded ln_loaded
        hT_ps hT_copied wr_loaded logit_ps logit_read max_ready rexp_done aff_ready affT_ps affT_copied slotT_ready slot_ps slots_ready
        sel_ready xin_ps xin_copied selT_ps selT_copied h_pair_ps silu_pair hid_ready hidT_ps hidT_copied y_pair_ps ye_copied sc_ps acc_added
        acc_init ln2_var ln2_std ln2_ready""".split()
        sems = {n: sem(n) for n in names}
        slice_loaded = [sem(f"slice_loaded_{i}") for i in range(NW)]
        out_stored = [sem(f"out_stored_{i}") for i in range(2)]
        w_loaded = [[sem(f"expert_{k}_{i}_loaded") for i in range(2)] for k in range(6)]
        w_used = [sem(f"expert_{k}_used") for k in range(6)]
        s = type("Sems", (), sems)

        w_rows = {n: w_dram[n] for n in w_dram}
        block = ctx.enter_context(nc.Block())

        @block.sync
        def _(sp):
            sp.dma_start(x_nat, A["x"][0].rearrange("(t p) d -> p t d", p=P)).then_inc(s.x_loaded, 16)

            def released(i):
                if i < 3:
                    return ((s.u_ps, 4), (s.u_ps, 6), (s.dt_ps, 1))[i]
                if i < FIRST_Z:
                    return s.xbc_ps, 4 * (i - 2)
                if i < FIRST_MIX:
                    return s.z_ps, TT * (i - FIRST_Z + 1)
                half, j = divmod(i - FIRST_MIX, 6)
                if j == 1:
                    return s.slice_used, half + 1
                return s.mix_ps, TT * (5 * half + (j if j == 0 else j - 1) + 1)

            for i, (name, k0, nk, c0, w) in enumerate(SL):
                if i >= NW:
                    sp.wait_ge(*released(i - NW))
                src = w_rows[name].rearrange("(k p) n -> p k n", p=P)[:, k0:k0 + nk, c0:c0 + w]
                sp.dma_start(wring[:, i % NW, 0:nk, 0:w], src).then_inc(slice_loaded[i % NW], 16)

            sp.wait_ge(s.wo_ps, 2)
            sp.dma_start(x_res, A["x"][0].rearrange("(t p) d -> p t d", p=P)).then_inc(s.xres_loaded, 16)
            for i, name in enumerate(("ln1_g", "ln1_b")):
                sp.dma_start(lnrow[:, i, :], A[name][0].partition_broadcast(P)).then_inc(s.ln_loaded, 16)
            sp.wait_ge(s.h_ready, TT)
            sp.dma_start(w_r, A["w_router"][0].rearrange("(k p) e -> p k e", p=P)).then_inc(s.wr_loaded, 16)
            for i, name in enumerate(("ln2_g", "ln2_b")):
                sp.dma_start(lnrow[:, i, :], A[name][0].partition_broadcast(P)).then_inc(s.ln_loaded, 16)
            w_e = [A["w_e1"][0], A["w_e3"][0], A["w_e2"][0]]
            with sp.Fori(0, EXPERTS // 4) as it:
                for u in range(2):
                    for c in range(NCH):
                        i = NCH * u + c
                        for kind in range(6):
                            which, e = divmod(kind, 2)
                            w = w_e[which][bass.ds(4 * it + 2 * u + e, 1)].rearrange("a m n -> (a m) n")
                            if which < 2:
                                src = w.rearrange("(k p) f -> p k f", p=P)[:, :, FC * c:FC * c + FC]
                                dst = ring[:, kind, i % 2].rearrange("p (k f) -> p k f", k=KT)
                            else:
                                src = w[FC * c:FC * c + FC].rearrange("(j p) d -> p j d", p=P)
                                dst = ring[:, kind, i % 2].rearrange("p (j d) -> p j d", j=2)
                            sp.wait_ge(w_used[kind], 2 * NCH * it + i + 1)
                            sp.dma_start(dst, src).then_inc(w_loaded[kind][i % 2], 16)

        @block.gpsimd
        def _(pool):
            n = Steps(pool, s.pool_step)
            for d, side in enumerate("fb"):
                pool.dma_start(par_raw[:, 3 * d, :], A["s5_a_re_" + side][0].rearrange("(g b) p -> g (b p)", b=2)).then_inc(s.params_loaded, 16)
                pool.dma_start(par_raw[:, 3 * d + 1, :], A["s5_a_im_" + side][0].rearrange("(g b) p -> g (b p)", b=2)).then_inc(s.params_loaded, 16)
                pool.dma_start(ls_raw[:, d, :], A["s5_log_step_" + side][0].rearrange("(g b) -> g b", b=2)).then_inc(s.params_loaded, 16)
            for r, name in enumerate(("s5_b_re", "s5_b_im")):
                pool.dma_start(b_raw[:, r], A[name][0].rearrange("(g b) p k -> (b p) g k", b=2)).then_inc(s.params_loaded, 16)
            for r, name in enumerate(("s5_c_re", "s5_c_im")):
                for q in range(GP // 8):
                    for b in range(2):
                        pool.dma_start(c_nat[:, q, r, b * S5_P:(b + 1) * S5_P],
                                       A[name][0].rearrange("(g b) k p -> b g k p", b=2)[b, 8 * q:8 * q + 8]).then_inc(s.params_loaded, 16)
            pool.dma_start(vec_a[0:100], A["conv_w"][0].rearrange("k (t p) -> (k t) p", p=P)).then_inc(s.params_loaded, 16)
            pool.dma_start(vec_a[100:120], A["conv_b"][0].rearrange("(t p) -> t p", p=P)).then_inc(s.params_loaded, 16)
            pool.dma_start(vec_b, A["ssd_norm_g"][0].rearrange("(t p) -> t p", p=P)).then_inc(s.params_loaded, 16)
            pool.dma_start(vec_d, A["s5_d"][0].rearrange("(g j) -> g j", j=2 * S5_K)).then_inc(s.params_loaded, 16)
            for d, side in enumerate("fb"):
                c = slice(d * HEADS, (d + 1) * HEADS)
                pool.dma_start(dt_bias[:, c], A["ssd_dt_bias_" + side][0].partition_broadcast(P)).then_inc(s.broadcasts_loaded, 16)
                pool.dma_start(a_neg[:, c], A["ssd_a_log_" + side][0].partition_broadcast(P)).then_inc(s.broadcasts_loaded, 16)
            pool.dma_start(d_row, A["ssd_d"][0].partition_broadcast(P)).then_inc(s.broadcasts_loaded, 16)
            n.link(pool.memset(ones, 1.0))
            pool.memset(eps_col, EPS).then_inc(s.consts_ready, 1)
            for m, step, op in ((ident, 1, ALU.is_equal), (m_le, 1, ALU.is_ge), (m_gt, -1, ALU.is_gt), (m_ge, -1, ALU.is_ge), (m_lt, 1, ALU.is_gt)):
                pool.affine_select(out=m, in_=ones, pattern=[[step, P]], compare_op=op, fill=0.0, base=0,
                                   channel_multiplier=-step).then_inc(s.consts_ready, 1)
            pool.iota(chunk_no, pattern=[[1, NC]], base=0, channel_multiplier=0,
                      allow_small_or_imprecise_dtypes=True).then_inc(s.consts_ready, 1)
            pool.iota(slot_no, pattern=[[1, CAP]], base=0, channel_multiplier=0,
                      allow_small_or_imprecise_dtypes=True).then_inc(s.consts_ready, 1)
            for c in range(S5_W // P):
                pool.wait_ge(s.u_copied, c + 1)
                pool.dma_start(u_dram[P * c:P * (c + 1)], uT[:, c, :].rearrange("p (s c) -> p s c", s=T)).then_inc(s.u_stored, 16)
            pool.wait_ge(s.u_stored, 16 * (S5_W // P))
            for b in range(2):
                for t in range(T):
                    r0 = b * T * S5_K + t * S5_K
                    pool.dma_start(U[r0:r0 + S5_K], u_dram.rearrange("(g b j) s c -> b s j g c", b=2, j=S5_K)[b, t]).then_inc(s.u_loaded, 16)
            for q in range(NQ + 1):
                if q < NQ:
                    pool.wait_ge(s.toep_built, q + 1)
                    pool.dma_start(toep_dram.rearrange("(g j) w -> j g w", j=2 * S5_K)[:, QB * q:QB * q + QB, :],
                                   toep[:, q % 2].rearrange("p g i k -> p g (i k)")).then_inc(s.toep_stored, 16)
                    pool.wait_ge(s.toep_stored, 16 * (q + 1))
                    pool.wait_ge(s.m_cleared, 1)
                    for b in range(2):
                        for t in range(T):
                            r0 = b * T * S5_K + t * S5_K
                            src = toep_dram.rearrange("(g b j) w -> b j g w", b=2, j=S5_K)[
                                b, :, QB * q:QB * q + QB, (T - 1 - t) * S5_K:(2 * T - 1 - t) * S5_K]
                            pool.dma_start(M[r0:r0 + S5_K, QB * q:QB * q + QB, b * T * S5_K:(b + 1) * T * S5_K], src).then_inc(s.toep_loaded, 16)
                    pool.wait_ge(s.toep_loaded, 16 * 2 * T * (q + 1))
                if q >= 1:
                    pool.wait_ge(s.y5_copied, q)
                    for b in range(2):
                        for t in range(T):
                            r0 = b * T * S5_K + t * S5_K
                            dst = y_dram.rearrange("(g b k) t c -> b t k g c", b=2, k=S5_K)[b, t, :, QB * (q - 1):QB * q, :]
                            pool.dma_start(dst, y5[r0:r0 + S5_K, (q - 1) % 2, :].rearrange("p (g c) -> p g c", g=QB)).then_inc(s.y5_stored, 16)
                    pool.wait_ge(s.y5_stored, 16 * 2 * T * q)
            pool.dma_start(ty5, y_dram.rearrange("(n p) t c -> p n (t c)", p=P)).then_inc(s.yT5_loaded, 16)
            pool.wait_ge(s.nat_copied, 16)
            pool.wait_ge(s.silu_done, 20)
            for i in range(GROUPS * TT):
                g, c = divmod(i, TT)
                f, b = slice(HG * g, HG * g + HG), slice(HEADS + HG * g, HEADS + HG * g + HG)
                if i >= 1:
                    pool.wait_ge(s.mats_ready, 2 * i)
                    pool.wait_ge(s.segm_ps, i)
                pool.tensor_tensor(rhs_f, first(m_le, HG), last(da[:, c, f], P), ALU.mult)
                pool.tensor_tensor(rhs_b, first(m_ge, HG), last(da[:, c, b], P), ALU.mult).then_inc(s.mats_ready, 1)
                if i >= 1:
                    pool.wait_ge(s.g_ready, i)
                pool.tensor_tensor(uf, first(m_le, HG), last(dtime[:, c, f], P), ALU.mult)
                n.link(pool.tensor_tensor(dmat, first(m_ge, HG), last(dtime[:, c, b], P), ALU.mult))
                pool.tensor_tensor(dmat, dmat, uf, ALU.add).then_inc(s.mats_ready, 1)

        @block.scalar
        def _(act):
            n = Steps(act, s.act_step)

            def f(out, in_, func, **kw):
                return act.activation(out, in_, func, **kw)

            for k in range(KT):
                act.wait_ge(s.xT_ps, k + 1)
                f(xT[:, k, :], ps[:, k % 2, :], ACT.Copy).then_inc(s.xT_copied, 1)
            for c in range(S5_W // P):
                act.wait_ge(s.u_ps, c + 1)
                f(uT[:, c, :].rearrange("p (s c) -> p c s", s=T), ps[:, c % 2, :].rearrange("p (c s) -> p c s", s=T),
                  ACT.Copy).then_inc(s.u_copied, 1)
            act.wait_ge(s.par_ready, 1)
            f(small[:, 0], par[:, :, 2, :], ACT.Exp).then_inc(s.step_exp, 1)
            act.wait_ge(s.lr_ready, 1)
            f(small[:, 3], small[:, 1], ACT.Tanh, scale=0.5).then_inc(s.tanh_done, 1)
            act.wait_ge(s.theta_ready, 1)
            f(small[:, 5], small[:, 4], ACT.Sin)
            f(small[:, 6], small[:, 4], ACT.Sin, scale=0.5).then_inc(s.sin_done, 1)
            act.wait_ge(s.dt_abs, 1)
            f(w_end[:, :, :], w_end[:, :, :], ACT.Exp, scale=-1.0).then_inc(s.dt_exp, 1)
            act.wait_ge(s.dt_exp, 1)
            f(w_end[:, :, :], w_end[:, :, :], ACT.Ln, bias=ones[:, 0:1]).then_inc(s.dt_ln, 1)
            act.wait_ge(s.broadcasts_loaded, 80)
            f(a_neg, a_neg, ACT.Exp).then_inc(s.dt_ln, 1)
            act.wait_ge(s.seg_ps, 1)
            H = HEADS
            sg = ps[:, 5, 0:16 * H].rearrange("p (k c h) -> p k c h", k=4, c=TT)
            f(e_cs[:, :, 0:H], sg[:, 0], ACT.Exp)
            f(e_cs[:, :, H:2 * H], sg[:, 1], ACT.Exp)
            f(w_end[:, :, 0:H], sg[:, 2], ACT.Exp)
            f(w_end[:, :, H:2 * H], sg[:, 3], ACT.Exp)
            f(e_all, ps[:, 6, 0:8 * H].rearrange("p (c h) -> p c h", c=TT), ACT.Exp).then_inc(s.seg_exp, 1)

            def block_diagonal(q):
                act.wait_ge(s.vw_ready, q + 1)
                if q >= 1:
                    act.wait_ge(s.bd_ready, q)
                    act.wait_ge(s.wT_ps, QB * q)
                if q >= 2:
                    act.wait_ge(s.y5_ps, q - 1)
                for b in range(2):
                    p, c = slice(64 * b, 64 * b + 64), slice(64 * b, 64 * b + 64)
                    for d in range(2):
                        i0 = S5_K if d == 0 else 0
                        f(vbd[p, q % 2, :, d, :, c], vc[p, q % 2, :, d, :, i0:i0 + 64], ACT.Copy)
                        r = f(wbd[p, :, d, :, c], wc[p, :, d, :, :], ACT.Copy)
                r.then_inc(s.bd_ready, 1)

            def gelu(q):
                act.wait_ge(s.y5_ps, q + 1)
                if q >= 2:
                    act.wait_ge(s.y5_stored, 16 * 2 * T * (q - 1))
                f(y5[:, q % 2, :], ps[:, 7, :], ACT.Gelu_apprx_tanh).then_inc(s.y5_copied, 1)

            act.wait_ge(s.m_cleared, 1)
            block_diagonal(0)
            for q in range(NQ):
                for j in range(QB):
                    i = QB * q + j
                    act.wait_ge(s.wT_ps, i + 1)
                    if i >= 2:
                        act.wait_ge(s.F_ps, i - 1)
                    f(wT[:, i % 2].rearrange("p a b -> p (a b)"), ps[:, 5 + i % 2, :], ACT.Copy).then_inc(s.wT_copied, 1)
                for d in range(2):
                    act.wait_ge(s.angle_ready, 2 * q + d + 1)
                    f(sin_t[:, d].rearrange("p g c -> p (g c)"), tph, ACT.Sin)
                    f(thf, tph, ACT.Sin, scale=0.5).then_inc(s.tab_sin, 1)
                if q + 1 < NQ:
                    block_diagonal(q + 1)
                if q >= 1:
                    gelu(q - 1)
            gelu(NQ - 1)
            act.wait_ge(s.yT5_loaded, 16)
            for c in range(S5_W // P):
                f(ysT[:, c, :].rearrange("p (c s) -> p c s", s=T), ty5[:, c, :].rearrange("p (s c) -> p c s", s=T),
                  ACT.Copy).then_inc(s.ysT_ready, 1)
            for b in range(XBC // 512 + 1):
                for j in range(4):
                    i = 4 * b + j
                    if i < 20:
                        act.wait_ge(s.xbc_ps, i + 1)
                        if b >= 1:
                            act.wait_ge(s.conv_done, 4 * b)
                        f(xraw[:, j, 2:2 + SEQ], ps[:, i % 2, :], ACT.Copy).then_inc(s.xbc_raw, 1)
                for j in range(4):
                    i = 4 * (b - 1) + j
                    if 0 <= i < 16:
                        act.wait_ge(s.nat_ps, i + 1)
                        src = ps[:, 2 + i % 2, :].rearrange("p (c w) -> p c w", c=TT)
                        dst = xs[:, :, P * i:P * i + P] if i < 12 else bn[:, :, P * (i - 12):P * (i - 11)]
                        f(dst, src, ACT.Copy).then_inc(s.nat_copied, 1)
                for j in range(4):
                    i = 4 * b + j
                    if i < 20:
                        act.wait_ge(s.conv_done, i + 1)
                        if 4 <= i < 12:
                            act.wait_ge(s.nat_ps, i - 3)
                        dst = xc[:, j, :] if i < 12 else (bT[:, i - 12, :] if i < 16 else cT[:, i - 16, :])
                        f(dst, cacc[:, j, :], ACT.Silu).then_inc(s.silu_done, 1)
            for g in range(GROUPS):
                for c in range(TT):
                    act.wait_ge(s.z_ps, g * TT + c + 1)
                    if g >= 2 and c == 0:
                        act.wait_ge(s.gate_ready, (g - 1) * TT)
                    f(zg[:, g % 2, c, :], ps[:, c % 2, 0:GI], ACT.Silu).then_inc(s.z_silu, 1)
                for c in range(TT):
                    i = g * TT + c
                    act.wait_ge(s.segm_ps, i + 1)
                    if i >= 1:
                        act.wait_ge(s.g_ready, i)
                    f(emat.rearrange("p (a b) q -> p a (b q)", a=2), ps[:, 2:4, 0:GI], ACT.Exp).then_inc(s.segm_exp, 1)
                    act.wait_ge(s.gate_ready, i + 1)
                    f(rms[:, i % 2, 1:2], rms[:, i % 2, 0:1], ACT.Sqrt, scale=1.0 / GI, bias=eps_col).then_inc(s.rms_sqrt, 1)
                    for j in range(3):
                        act.wait_ge(s.yt_ps, i + 1)
                        f(yT[:, 3 * g + j, P * c:P * c + P], ps[:, i % 2, P * j:P * (j + 1)], ACT.Copy,
                          scale=norm_g[:, 3 * g + j:3 * g + j + 1]).then_inc(s.yt_copied, 1)
            for m in range(10):
                k = m % 5
                if k in (0, 2, 3):
                    dst = {0: sg_a, 2: sg_b, 3: sg_u}[k]
                    for c in range(TT):
                        act.wait_ge(s.mix_ps, TT * m + c + 1)
                        if m >= 5:
                            act.wait_ge(s.mix_ready, TT)
                        f(dst[:, c, :], ps[:, 4 * (m % 2) + c, :], ACT.Sigmoid).then_inc(s.mix_sig, 1)
            for c in range(TT):
                for j in range(2):
                    act.wait_ge(s.mixT_ps, 2 * c + j + 1)
                    if c >= 2:
                        act.wait_ge(s.wo_ps, 2 * (c - 1))
                    f(mixT[:, c % 2, 4 * j:4 * j + 4, :].rearrange("p a b -> p (a b)"), ps[:, j, :], ACT.Copy).then_inc(s.mixT_copied, 1)
                if c >= 1:
                    act.wait_ge(s.var_ready, c)
                    f(mv[:, 2:3], mv[:, 1:2], ACT.Sqrt, bias=eps_col).then_inc(s.std_ready, 1)
            act.wait_ge(s.var_ready, TT)
            f(mv[:, 2:3], mv[:, 1:2], ACT.Sqrt, bias=eps_col).then_inc(s.std_ready, 1)
            for k in range(KT):
                act.wait_ge(s.hT_ps, k + 1)
                f(hT[:, k, :], ps[:, k % 2, :], ACT.Copy).then_inc(s.hT_copied, 1)
            act.wait_ge(s.max_ready, 1)
            for c in range(TT):
                r = f(ex_t[:, c, :], logit[:, c, :], ACT.Exp, bias=sm[:, 1, c:c + 1], accum_out=sm[:, 2, c:c + 1])
            r.then_inc(s.rexp_done, 1)
            act.wait_ge(s.affT_ps, 1)
            f(affT, ps[0:EXPERTS, 3, :], ACT.Copy).then_inc(s.affT_copied, 1)
            act.wait_ge(s.slot_ps, 1)
            f(slotv, ps[:, 4, 0:TT * EXPERTS].rearrange("p (c e) -> p c e", c=TT), ACT.Copy).then_inc(s.slots_ready, 1)
            with act.Fori(0, EXPERTS // 4) as it:
                for u in range(2):
                    for j in range(2):
                        act.wait_ge(s.xin_ps, 4 * it + 2 * u + j + 1)
                        f(xin[:, 4 * j:4 * j + 4, :].rearrange("p a b -> p (a b)"), ps[:, 5 + j, :], ACT.Copy).then_inc(s.xin_copied, 1)
                    act.wait_ge(s.selT_ps, 2 * it + u + 1)
                    f(selgT.rearrange("p a b -> p (a b)"), ps[:, 7, :], ACT.Copy).then_inc(s.selT_copied, 1)
                    for c in range(NCH):
                        i = NCH * u + c
                        act.wait_ge(w_used[3], 2 * NCH * it + i + 3)
                        f(s_h1[:, i % 2, :], ps[:, i % 2, 0:256], ACT.Silu).then_inc(s.silu_pair, 1)
                        act.wait_ge(s.hidT_ps, 2 * NCH * it + i + 1)
                        f(hidT[:, i % 2].rearrange("p a b -> p (a b)"), ps[:, 2, 256 * (i % 2):256 * (i % 2) + 256], ACT.Copy).then_inc(s.hidT_copied, 1)
                    act.wait_ge(w_used[5], 2 * NCH * it + NCH * (u + 1) + 2)
                    f(ye, ps[:, 3:5, :].rearrange("p a b -> p (a b)"), ACT.Copy).then_inc(s.ye_copied, 1)
            for c in range(TT):
                act.wait_ge(s.ln2_var, c + 1)
                f(mv[:, 2:3], mv[:, 1:2], ACT.Sqrt, bias=eps_col).then_inc(s.ln2_std, 1)
                act.wait_ge(s.ln2_ready, c + 1)
                act.dma_start(out[0].rearrange("(t p) d -> t p d", p=P)[c], lnout if c % 2 else lnout2).then_inc(out_stored[c % 2], 16)
            for half in out_stored:
                act.wait_ge(half, 16 * TT // 2)

        @block.tensor
        def _(pe):
            def mm(out, lhsT, rhs, a, z):
                return pe.matmul(out, lhsT, rhs, start=a, stop=z)

            used = [0]

            def slice_wait():
                i = used[0]
                pe.wait_ge(slice_loaded[i % NW], 16 * (i // NW + 1))
                used[0] += 1
                return wring[:, i % NW]

            def before(m, c):
                gates, products = (0, 2, 3, 5, 7, 8), (1, 4, 6, 9)
                if m in gates:
                    return s.mix_sig, gates.index(m) * TT + c + 1
                return s.mix_read, products.index(m) * TT + c + 1

            pe.wait_ge(s.consts_ready, 8)
            pe.wait_ge(s.x_loaded, 16)
            for k in range(KT):
                if k >= 2:
                    pe.wait_ge(s.xT_copied, k - 1)
                for c in range(TT):
                    r = pe.transpose(ps[:, k % 2, P * c:P * c + P], x_nat[:, c, P * k:P * k + P], ident)
                r.then_inc(s.xT_ps, 1)
            pe.wait_ge(s.params_loaded, 16 * PARAMS)
            pe.wait_ge(s.ls_filled, 1)
            for r in range(2):
                for q in range(GP // 8):
                    pe.transpose(ps[:, 2 + r, P * q:P * q + P], c_nat[:, q, r, :], ident)
            for i in range(6):
                pe.transpose(ps[:, 4, GP * i:GP * i + GP], par_raw[:, i, :], ident[0:GP, 0:GP])
            pe.transpose(ps[:, 4, 144:264], vec_a, ident[0:120, 0:120])
            pe.transpose(ps[:, 4, 264:276], vec_b, ident[0:12, 0:12])
            pe.transpose(ps[0:2 * S5_K, 4, 276:300], vec_d, ident[0:GP, 0:GP]).then_inc(s.vec_ps, 1)
            pe.wait_ge(s.xT_copied, KT)
            for i in range(S5_W // P):
                if i in (0, 4):
                    w = slice_wait()
                if i >= 2:
                    pe.wait_ge(s.u_copied, i - 1)
                for k in range(KT):
                    r = mm(ps[:, i % 2, :], w[:, k, P * (i % 4):P * (i % 4) + P], xT[:, k, :], k == 0, k == KT - 1)
                r.then_inc(s.u_ps, 1)
            w = slice_wait()
            for c in range(TT):
                for k in range(KT):
                    r = mm(ps[:, 5, 48 * c:48 * c + 48], xT[:, k, P * c:P * c + P], w[:, k, 0:48], k == 0, k == KT - 1)
            r.then_inc(s.dt_ps, 1)
            pe.wait_ge(s.da_ready, 1)
            H = HEADS
            for i, (m, c0) in enumerate(((m_le, 0), (m_ge, H), (m_gt, 0), (m_lt, H))):
                mm(ps[:, 5, 96 * i:96 * i + 96].rearrange("p (c h) -> p c h", c=TT), m, da[:, :, c0:c0 + H], True, True)
            mm(ps[:, 6, 0:8 * H].rearrange("p (c h) -> p c h", c=TT), ones, da, True, True).then_inc(s.seg_ps, 1)

            def toeplitz(q):
                pe.wait_ge(s.vw_ready, q + 1)
                if q >= 1:
                    pe.wait_ge(s.toep_built, q)
                for d in range(2):
                    i0 = 0 if d == 0 else S5_K
                    for g in range(QB):
                        at = (d * QB + g) * 64
                        for r in range(2):
                            ins = mm(ps[0:32, 4, at:at + 64], bpad[:, g, d, r, :], vc[:, q % 2, g, d, r, i0:i0 + 64], r == 0, r == 1)
                ins.then_inc(s.toep_ps, 1)

            def states(q):
                pe.wait_ge(s.bd_ready, q + 1)
                pe.wait_ge(s.u_loaded, 16 * 2 * T)
                if q >= 1:
                    pe.wait_ge(s.F_read, 2 * q)
                for g in range(QB + 1):
                    if g < QB:
                        i = QB * q + g
                        if i >= 2:
                            pe.wait_ge(s.wT_copied, i - 1)
                        for k in range(4):
                            r = pe.transpose(ps[:, 5 + i % 2, P * k:P * k + P], wbd[:, g, k // 2, k % 2, :], ident)
                        r.then_inc(s.wT_ps, 1)
                    if g >= 1:
                        i = QB * q + g - 1
                        pe.wait_ge(s.wT_copied, i + 1)
                        for k in range(4):
                            r = mm(ps[:, k, P * (g - 1):P * g], wT[:, i % 2, k, :], U[:, i, :], True, True)
                        r.then_inc(s.F_ps, 1)

            def outputs(q):
                pe.wait_ge(s.X_ready, 2 * (q + 1))
                pe.wait_ge(s.toep_loaded, 16 * 2 * T * (q + 1))
                if q >= 1:
                    pe.wait_ge(s.y5_copied, q)
                for g in range(QB):
                    o = ps[:, 7, P * g:P * g + P]
                    mm(o, M[:, QB * q + g, :], U[:, QB * q + g, :], True, False)
                    for k in range(4):
                        r = mm(o, vbd[:, q % 2, g, k // 2, k % 2, :], X[:, q % 2, k // 2, k % 2, g, :], False, k == 3)
                r.then_inc(s.y5_ps, 1)

            pe.wait_ge(s.seg_exp, 1)
            for q in range(NQ):
                toeplitz(q)
                states(q)
                if q >= 1:
                    outputs(q - 1)
            outputs(NQ - 1)
            pe.wait_ge(s.ysT_ready, S5_W // P)
            for b in range(XBC // 512 + 1):
                if b < XBC // 512:
                    w = slice_wait()
                    for j in range(4):
                        i = 4 * b + j
                        if i >= 2:
                            pe.wait_ge(s.xbc_raw, i - 1)
                        for k in range(KT):
                            r = mm(ps[:, i % 2, :], w[:, k, P * j:P * j + P], xT[:, k, :], k == 0, k == KT - 1)
                        r.then_inc(s.xbc_ps, 1)
                for j in range(4):
                    i = 4 * (b - 1) + j
                    if 0 <= i < 16:
                        pe.wait_ge(s.silu_done, i + 1)
                        if i >= 2:
                            pe.wait_ge(s.nat_copied, i - 1)
                        src = xc[:, j, :] if i < 12 else bT[:, i - 12, :]
                        for c in range(TT):
                            r = pe.transpose(ps[:, 2 + i % 2, P * c:P * c + P], src[:, P * c:P * c + P], ident)
                        r.then_inc(s.nat_ps, 1)
            pe.wait_ge(s.silu_done, 20)
            pe.wait_ge(s.nat_copied, 16)
            for g in range(GROUPS):
                w = slice_wait()
                for c in range(TT):
                    if g * TT + c >= 2:
                        pe.wait_ge(s.z_silu, g * TT + c - 1)
                    if g >= 1 and c < 2:
                        pe.wait_ge(s.yt_copied, 3 * TT * g)
                    for k in range(KT):
                        r = mm(ps[:, c % 2, 0:GI], xT[:, k, P * c:P * c + P], w[:, k, 0:GI], k == 0, k == KT - 1)
                    r.then_inc(s.z_ps, 1)
                if g >= 1:
                    pe.wait_ge(s.y_read, TT * g)
                for j in range(TT - 1):
                    for d, c in ((0, j), (1, TT - 1 - j)):
                        i = 6 * g + 2 * j + d
                        pe.wait_ge(s.xw_ready, i + 1)
                        if i >= 2:
                            pe.wait_ge(s.carried, i - 1)
                        mm(ps[:, 6 + d, 0:GI], bn[:, c, P * g:P * g + P], xw[:, d, :], True, True).then_inc(s.st_ps, 1)
                for c in range(TT):
                    i = g * TT + c
                    q = slice(P * c, P * c + P)
                    if i >= 1:
                        pe.wait_ge(s.g_ready, i)
                    mm(ps[:, 4, 0:P], bT[:, g, q], cT[:, g, q], True, True).then_inc(s.cb_ps, 1)
                    pe.wait_ge(s.mats_ready, 2 * i + 1)
                    if i >= 1:
                        pe.wait_ge(s.segm_exp, i)
                    for a in range(2):
                        o = ps[:, 2 + a, 0:GI].rearrange("p (h q) -> p h q", h=3)
                        mm(o, m_gt, rhs_f[:, 3 * a:3 * a + 3, :], True, False)
                        r = mm(o, m_lt, rhs_b[:, 3 * a:3 * a + 3, :], False, True)
                    r.then_inc(s.segm_ps, 1)
                    pe.wait_ge(s.carried, 6 * (g + 1))
                    if i >= 1:
                        pe.wait_ge(s.y_read, i)
                    if c >= 1:
                        mm(ps[:, 6, 0:GI], cT[:, g, q], st[:, 0, c, :], True, True)
                    if c < TT - 1:
                        mm(ps[:, 7, 0:GI], cT[:, g, q], st[:, 1, c, :], True, True)
                    pe.wait_ge(s.g_ready, i + 1)
                    for j in range(HG):
                        h0 = GI * g + HEADDIM * j
                        r = mm(ps[:, 5, HEADDIM * j:HEADDIM * j + HEADDIM], gmat[:, j, :], xs[:, c, h0:h0 + HEADDIM], True, True)
                    r.then_inc(s.yd_ps, 1)
                    pe.wait_ge(s.yn_ready, i + 1)
                    if i >= 1:
                        pe.wait_ge(s.yt_copied, 3 * i)
                    for j in range(3):
                        r = pe.transpose(ps[:, i % 2, P * j:P * (j + 1)], ty[:, 4, P * j:P * j + P], ident)
                    r.then_inc(s.yt_ps, 1)
            pe.wait_ge(s.yt_copied, 3 * GROUPS * TT)
            for m in range(10):
                k = m % 5
                lhs, halves = {0: (xT, 1), 1: (yT, 2), 2: (xT, 1), 3: (ysT, 1), 4: (ysT, 1)}[k]
                nk = {0: KT, 1: 6, 2: KT, 3: 6, 4: 6}[k]
                for half in range(halves):
                    w = slice_wait()
                    for c in range(TT):
                        if half == 0 and m >= 2:
                            pe.wait_ge(*before(m - 2, c))
                        for kk in range(nk):
                            r = mm(ps[:, 4 * (m % 2) + c, :], lhs[:, 6 * half + kk, P * c:P * c + P], w[:, kk, :],
                                   half == 0 and kk == 0, half == halves - 1 and kk == nk - 1)
                        if half == halves - 1:
                            r.then_inc(s.mix_ps, 1)
                        elif c == TT - 1:
                            r.then_inc(s.slice_used, 1)
            pe.wait_ge(s.mix_ready, 2 * TT)
            pe.wait_ge(s.mix_sig, 6 * TT)
            w0 = slice_wait()
            w1 = slice_wait()
            for c in range(TT):
                if c >= 1:
                    pe.wait_ge(s.mixT_copied, 2 * c)
                for j in range(2):
                    for k in range(4):
                        kk = 4 * j + k
                        r = pe.transpose(ps[:, j, P * k:P * k + P], mix[:, c, P * kk:P * kk + P], ident)
                    r.then_inc(s.mixT_ps, 1)
                pe.wait_ge(s.mixT_copied, 2 * (c + 1))
                if c >= 2:
                    pe.wait_ge(s.wo_read, 2 * (c - 1))
                for j, w in enumerate((w0, w1)):
                    for k in range(KT):
                        r = mm(ps[:, 2 + 2 * (c % 2) + j, :], mixT[:, c % 2, k, :], w[:, k, :], k == 0, k == KT - 1)
                    r.then_inc(s.wo_ps, 1)
            pe.wait_ge(s.h_ready, TT)
            for k in range(KT):
                if k >= 2:
                    pe.wait_ge(s.hT_copied, k - 1)
                for c in range(TT):
                    r = pe.transpose(ps[:, k % 2, P * c:P * c + P], h[:, c, P * k:P * k + P], ident)
                r.then_inc(s.hT_ps, 1)
            pe.wait_ge(s.hT_copied, KT)
            pe.wait_ge(s.wr_loaded, 16)
            for c in range(TT):
                for k in range(KT):
                    r = mm(ps[:, 2, EXPERTS * c:EXPERTS * c + EXPERTS], hT[:, k, P * c:P * c + P], w_r[:, k, :], k == 0, k == KT - 1)
            r.then_inc(s.logit_ps, 1)
            pe.wait_ge(s.aff_ready, 1)
            for c in range(TT):
                r = pe.transpose(ps[0:EXPERTS, 3, P * c:P * c + P], aff[:, c, :], ident)
            r.then_inc(s.affT_ps, 1)
            pe.wait_ge(s.slotT_ready, 1)
            for c in range(TT):
                r = pe.transpose(ps[:, 4, EXPERTS * c:EXPERTS * c + EXPERTS], cum[:, P * c:P * c + P], ident[0:EXPERTS, 0:EXPERTS])
            r.then_inc(s.slot_ps, 1)
            pe.wait_ge(s.acc_init, 1)
            for k in range(6):
                pe.nop().then_inc(w_used[k], 2)
            with pe.Fori(0, EXPERTS // 4) as it:
                for u in range(2):
                    pair = 2 * it + u
                    pe.wait_ge(s.sel_ready, pair + 1)
                    for j in range(2):
                        for k in range(4):
                            for c in range(TT):
                                kk = 4 * j + k
                                r = mm(ps[:, 5 + j, P * k:P * k + P], h[:, c, P * kk:P * kk + P],
                                       sel[:, c].rearrange("p a b -> p (a b)"), c == 0, c == TT - 1)
                        r.then_inc(s.xin_ps, 1)
                    for c in range(TT):
                        r = pe.transpose(ps[:, 7, P * c:P * c + P], selg[:, c].rearrange("p a b -> p (a b)"), ident)
                    r.then_inc(s.selT_ps, 1)
                    pe.wait_ge(s.xin_copied, 2 * pair + 2)

                    def hidden(i, which):
                        for e in range(2):
                            pe.wait_ge(w_loaded[2 * which + e][i % 2], 16 * NCH * it + 16 * (i // 2 + 1))
                        for k in range(KT):
                            for e in range(2):
                                w = ring[:, 2 * which + e, i % 2].rearrange("p (k f) -> p k f", k=KT)
                                r = mm(ps[64 * e:64 * e + 64, i % 2, FC * which:FC * which + FC],
                                       xin[:, k, 64 * e:64 * e + 64], w[:, k, :], k == 0, k == KT - 1)
                                if k == KT - 1:
                                    r.then_inc(w_used[2 * which + e], 1)
                        return r

                    def turn(i):
                        pe.wait_ge(s.hid_ready, 2 * NCH * it + i + 1)
                        for j in range(2):
                            r = pe.transpose(ps[:, 2, 256 * (i % 2) + P * j:256 * (i % 2) + P * j + P], hid[:, i % 2, P * j:P * j + P], ident)
                        r.then_inc(s.hidT_ps, 1)

                    def down(i, c):
                        pe.wait_ge(s.hidT_copied, 2 * NCH * it + i + 1)
                        for e in range(2):
                            pe.wait_ge(w_loaded[4 + e][i % 2], 16 * NCH * it + 16 * (i // 2 + 1))
                        for j in range(2):
                            for n in range(2):
                                for e in range(2):
                                    w = ring[:, 4 + e, i % 2].rearrange("p (j d) -> p j d", j=2)
                                    r = mm(ps[64 * e:64 * e + 64, 3 + n, :], hidT[:, i % 2, j, 64 * e:64 * e + 64],
                                           w[:, j, 512 * n:512 * n + 512], c == 0 and j == 0, c == NCH - 1 and j == 1)
                                    if j == 1 and n == 1:
                                        r.then_inc(w_used[4 + e], 1)

                    for c in range(NCH):
                        i = NCH * u + c
                        if i >= 2:
                            pe.wait_ge(s.hid_ready, 2 * NCH * it + i - 1)
                        hidden(i, 0)
                        if c >= 1:
                            turn(i - 1)
                        hidden(i, 1)
                        if c >= 1:
                            down(i - 1, c - 1)
                    turn(NCH * u + NCH - 1)
                    down(NCH * u + NCH - 1, NCH - 1)
                    pe.wait_ge(s.ye_copied, pair + 1)
                    pe.wait_ge(s.selT_copied, pair + 1)
                    for k in range(2 * TT):
                        c, j = divmod(k, 2)
                        if k >= 2:
                            pe.wait_ge(s.acc_added, 2 * TT * pair + k - 1)
                        mm(ps[:, 5 + k % 2, :], selgT[:, c, :], ye[:, 512 * j:512 * j + 512], True, True).then_inc(s.sc_ps, 1)
                    pe.wait_ge(s.acc_added, 2 * TT * pair + 2 * TT)

        @block.vector
        def _(dve):
            n = Steps(dve, s.dve_step)
            tt, ts, stt = dve.tensor_tensor, dve.tensor_scalar, dve.scalar_tensor_tensor

            def reduce_phase(out, x, k, tmp):
                n.link(ts(k, x, 1.0 / TWO_PI, ROUND, ALU.mult, ALU.add))
                n.link(ts(k, k, -ROUND, None, ALU.add))
                n.link(stt(tmp, k, -PI_1, x, ALU.mult, ALU.add))
                n.link(stt(out, k, -PI_2, tmp, ALU.mult, ALU.add))
                n.link(stt(tmp, k, -PI_3, out, ALU.mult, ALU.add))
                n.link(ts(out, tmp, PI_LIM, -PI_LIM, ALU.min, ALU.max))

            def cmul(o_re, o_im, a_re, a_im, b_re, b_im, t):
                tt(t[0], a_re, b_re, ALU.mult)
                tt(t[1], a_im, b_im, ALU.mult)
                tt(t[2], a_re, b_im, ALU.mult)
                n.link(tt(t[3], a_im, b_re, ALU.mult))
                tt(o_re, t[0], t[1], ALU.subtract)
                n.link(tt(o_im, t[2], t[3], ALU.add))

            dve.wait_ge(s.xT_ps, KT)
            n.done(dve.memset(vbd, 0.0))
            n.done(dve.memset(wbd, 0.0))
            n.done(dve.memset(bpad, 0.0))
            dve.memset(M, 0.0).then_inc(s.m_cleared, 1)
            dve.wait_ge(s.params_loaded, 16 * PARAMS)
            for d in range(2):
                r = dve.tensor_copy(par_raw[:, 3 * d + 2, :].rearrange("g (b p) -> g b p", b=2), last(ls_raw[:, d, :], S5_P))
            r.then_inc(s.ls_filled, 1)
            dve.wait_ge(s.vec_ps, 1)
            for r in range(2):
                n.done(dve.tensor_copy(c_map[:, r].rearrange("p g k -> p (g k)"), ps[:, 2 + r, 0:GP * S5_K]))
            n.done(dve.tensor_copy(conv_w, ps[:, 4, 144:244].rearrange("p (k t) -> p t k", k=CONV)))
            n.done(dve.tensor_copy(conv_b, ps[:, 4, 244:264]))
            n.done(dve.tensor_copy(norm_g, ps[:, 4, 264:276]))
            n.done(dve.tensor_copy(d_col, ps[0:32, 4, 276:300]))
            n.done(tt(eye2, ident[0:32, 0:16], ident[0:32, 16:32], ALU.add))
            dve.tensor_copy(par.rearrange("p a b c -> p (a b c)"), ps[:, 4, 0:6 * GP]).then_inc(s.par_ready, 1)
            dve.wait_ge(s.par_ready, 1)
            n.wait()
            n.done(tt(d_diag, first(eye2, GP), last(d_col, S5_K), ALU.mult))
            a_re, a_im = par[:, :, 0, :], par[:, :, 1, :]
            v = lambda i: small[:, i]
            dve.wait_ge(s.step_exp, 1)
            tt(v(1), a_re, v(0), ALU.mult).then_inc(s.lr_ready, 1)
            n.link(tt(v(2), a_im, v(0), ALU.mult))
            reduce_phase(v(4), v(2), v(7), v(8))
            dve.tensor_copy(v(9), v(4)).then_inc(s.theta_ready, 1)
            dve.wait_ge(s.tanh_done, 1)
            n.link(ts(v(10), v(3), -1.0, 1.0, ALU.mult, ALU.add))
            n.link(dve.reciprocal(v(11), v(10)))
            n.link(stt(v(12), v(3), 2.0, v(11), ALU.mult, ALU.mult))
            n.link(ts(v(13), v(12), 1.0, None, ALU.add))
            dve.wait_ge(s.sin_done, 1)
            n.link(stt(v(14), v(6), 2.0, v(6), ALU.mult, ALU.mult))
            n.link(ts(v(15), v(14), -1.0, 1.0, ALU.mult, ALU.add))
            n.link(tt(v(16), v(12), v(15), ALU.mult))
            n.done(tt(v(17), v(16), v(14), ALU.subtract))
            n.done(tt(v(18), v(13), v(5), ALU.mult))
            n.done(tt(v(19), v(13), v(15), ALU.mult))
            tt(v(20), a_re, a_re, ALU.mult)
            n.link(tt(v(21), a_im, a_im, ALU.mult))
            n.link(tt(v(22), v(20), v(21), ALU.add))
            n.done(dve.reciprocal(v(23), v(22)))
            n.done(ts(v(24), a_im, -1.0, None, ALU.mult))
            n.wait()
            cmul(v(25), v(26), v(17), v(18), a_re, v(24), [small[:, 27 + i] for i in range(4)])
            n.done(tt(v(25), v(25), v(23), ALU.mult))
            n.done(tt(v(26), v(26), v(23), ALU.mult))
            n.wait()
            tb = [vc.rearrange("p a b c d e -> p (a b c d e)")[:, GP * S5_K * i:GP * S5_K * (i + 1)].rearrange("p (g k) -> p g k", g=GP)
                  for i in range(4)]
            for d in range(2):
                q_re, q_im = last(small[:, 25, d], S5_K), last(small[:, 26, d], S5_K)
                cmul(bbar[:, d, 0], bbar[:, d, 1], q_re, q_im, b_raw[:, 0], b_raw[:, 1], tb)
            n.done(dve.memset(X, 0.0))
            pw = [[pt[:, 0, r, :, :, j] for r in range(2)] for j in range(T + 1)]
            n.done(dve.memset(pw[0][0], 1.0))
            n.done(dve.memset(pw[0][1], 0.0))
            n.done(dve.tensor_copy(pw[1][0], v(19)))
            n.done(dve.tensor_copy(pw[1][1], v(18)))
            n.wait()
            tp = [small[:, 27 + i] for i in range(4)]
            cmul(*pw[2], *pw[1], *pw[1], tp)
            cmul(*pw[3], *pw[2], *pw[1], tp)
            cmul(*pw[4], *pw[2], *pw[2], tp)
            for j in range(T + 1):
                for r in range(2):
                    n.done(dve.tensor_copy(pt[:, 1, r, :, :, T - j], pw[j][r]))
            n.link(tt(v(7), v(13), v(13), ALU.mult))
            n.link(tt(v(20), v(7), v(7), ALU.mult))
            n.link(ts(v(21), v(4), float(T), None, ALU.mult))
            reduce_phase(v(22), v(21), v(7), v(8))
            modulus, phase = v(20), v(22)

            dve.wait_ge(s.dt_ps, 1)
            dve.wait_ge(s.broadcasts_loaded, 80)
            n.link(tt(dtime, ps[:, 5, 0:TT * 2 * HEADS].rearrange("p (c h) -> p c h", c=TT), first(dt_bias, TT), ALU.add))
            stt(w_end, dtime, -1.0, dtime, ALU.mult, ALU.max).then_inc(s.dt_abs, 1)
            dve.wait_ge(s.dt_ln, 2)
            n.link(stt(dtime, dtime, 0.0, w_end, ALU.max, ALU.add))
            dve.scalar_tensor_tensor(da, dtime, -1.0, first(a_neg, TT), ALU.mult, ALU.mult).then_inc(s.da_ready, 1)
            dve.wait_ge(s.seg_exp, 1)
            tt(w_end, w_end, dtime, ALU.mult).then_inc(s.wend_ready, 1)

            def maps(q):
                gs = slice(QB * q, QB * q + QB)
                if q >= 1:
                    dve.wait_ge(s.toep_ps, q)
                if q >= 1:
                    dve.wait_ge(s.bd_ready, q)
                    dve.wait_ge(s.vw_ready, q)
                tv = [x.rearrange("p g c -> p (g c)")[:, 0:QB * 80].rearrange("p (g i k) -> p g i k", g=QB, k=S5_K) for x in (t1, t2)]
                tw = [x.rearrange("p g c -> p (g c)")[:, 0:QB * 64].rearrange("p (g i k) -> p g i k", g=QB, k=S5_K) for x in (sr, si)]
                for d in range(2):
                    pv, pwd = pt[:, d, :, d, gs, :], (pt[:, 1, :, 0, gs, 1:] if d == 0 else pt[:, 0, :, 1, gs, 0:T])
                    for src, cm, out, tmp, rows in ((pv, c_map, vc[:, q % 2], tv, T + 1), (pwd, bbar[:, d], wc, tw, T)):
                        c_re, c_im = (mid2(cm[:, r, gs, :], rows) for r in range(2))
                        p_re, p_im = (last(src[:, r], S5_K) for r in range(2))
                        o = [out[:, :, d, r, :].rearrange("p g (i k) -> p g i k", k=S5_K) for r in range(2)]
                        tt(tmp[0], p_re, c_re, ALU.mult)
                        n.link(tt(tmp[1], p_im, c_im, ALU.mult))
                        n.link(tt(o[0], tmp[0], tmp[1], ALU.subtract))
                        tt(tmp[0], p_re, c_im, ALU.mult)
                        n.link(tt(tmp[1], p_im, c_re, ALU.mult))
                        if out is wc:
                            n.link(tt(o[1], tmp[0], tmp[1], ALU.add))
                        else:
                            n.link(stt(out[:, :, d, 1, :], tmp[0].rearrange("p g i k -> p g (i k)"), -1.0,
                                       tmp[1].rearrange("p g i k -> p g (i k)"), ALU.mult, ALU.subtract))
                for b in range(2):
                    for d in range(2):
                        p = slice(64 * b, 64 * b + 64)
                        r = dve.tensor_copy(bpad[p, :, d, :, S5_K * b:S5_K * b + S5_K],
                                            bbar[p, d, :, gs, :].rearrange("p r g k -> p g r k"))
                r.then_inc(s.vw_ready, 1)

            def toeplitz_rows(q):
                dve.wait_ge(s.toep_ps, q + 1)
                if q >= 2:
                    dve.wait_ge(s.toep_stored, 16 * (q - 1))
                k = ps[0:32, 4, :].rearrange("p (d g i k) -> p d g i k", d=2, g=QB, k=S5_K)
                o = toep[:, q % 2]
                dve.tensor_copy(o[:, :, 0:T - 1, :], k[:, 1, :, 0:T - 1, :])
                dve.tensor_copy(o[:, :, T:, :], k[:, 0, :, 1:, :])
                n.link(tt(o[:, :, T - 1, :], k[:, 1, :, T - 1, :], d_diag[:, QB * q:QB * q + QB, :], ALU.add))
                tt(o[:, :, T - 1, :], o[:, :, T - 1, :], k[:, 0, :, 0, :], ALU.add).then_inc(s.toep_built, 1)

            def tables(q, d):
                gs = slice(QB * q, QB * q + QB)
                i = 2 * q + d
                if i >= 1:
                    dve.wait_ge(s.tab_sin, i)
                flat = lambda x: x.rearrange("p g c -> p (g c)")
                n.link(tt(trd.rearrange("p (g c) -> p g c", g=QB), last(phase[:, d, gs], NC), first(chunk_no, QB), ALU.mult))
                n.link(ts(trn, trd, 1.0 / TWO_PI, ROUND, ALU.mult, ALU.add))
                n.link(ts(trn, trn, -ROUND, None, ALU.add))
                n.link(stt(trd, trn, -PI_1, trd, ALU.mult, ALU.add))
                n.link(stt(trd, trn, -PI_2, trd, ALU.mult, ALU.add))
                n.link(stt(trd, trn, -PI_3, trd, ALU.mult, ALU.add))
                ts(tph, trd, PI_LIM, -PI_LIM, ALU.min, ALU.max).then_inc(s.angle_ready, 1)
                dve.wait_ge(s.tab_sin, i + 1)
                n.link(stt(flat(cos_t[:, d]), thf, -2.0, thf, ALU.mult, ALU.mult))
                n.link(ts(flat(cos_t[:, d]), flat(cos_t[:, d]), 1.0, None, ALU.add))

            def recur(q, d):
                dve.wait_ge(s.F_ps, QB * (q + 1))
                if q >= 2:
                    dve.wait_ge(s.y5_ps, q - 1)
                F = [ps[:, 2 * d + r, :].rearrange("p (g c) -> p g c", g=QB) for r in range(2)]
                if d == 1:
                    F = [x[:, :, ::-1] for x in F]
                n.link(dve.tensor_copy(decay, last(modulus[:, d, QB * q:QB * q + QB], NC)))
                n.done(dve.memset(decay[:, :, 0:1], 0.0))
                c, sn = cos_t[:, d], sin_t[:, d]
                flat = lambda x: x.rearrange("p g c -> p (g c)")
                tt(zr, F[0], c, ALU.mult)
                tt(zi, F[1], c, ALU.mult)
                tt(t1, F[1], sn, ALU.mult)
                n.link(tt(t2, F[0], sn, ALU.mult))
                tt(zr, zr, t1, ALU.add)
                tt(zi, zi, t2, ALU.subtract).then_inc(s.F_read, 1)
                dve.wait_ge(s.F_read, 2 * q + d + 1)
                dve.tensor_tensor_scan(flat(sr), flat(decay), flat(zr), 0.0, ALU.mult, ALU.add)
                n.link(dve.tensor_tensor_scan(flat(si), flat(decay), flat(zi), 0.0, ALU.mult, ALU.add))
                tt(zr, sr, c, ALU.mult)
                tt(zi, sr, sn, ALU.mult)
                tt(t1, si, sn, ALU.mult)
                n.link(tt(t2, si, c, ALU.mult))
                L = NC - 1
                for r, (x, y, op) in enumerate(((zr, t1, ALU.subtract), (zi, t2, ALU.add))):
                    o = X[:, q % 2, d, r]
                    o = o[:, :, 1:] if d == 0 else o[:, :, 0:L][:, :, ::-1]
                    ins = tt(o, x[:, :, 0:L], y[:, :, 0:L], op)
                ins.then_inc(s.X_ready, 1)
                dve.wait_ge(s.X_ready, 2 * q + d + 1)

            maps(0)
            for q in range(NQ):
                if q + 1 < NQ:
                    maps(q + 1)
                for d in range(2):
                    tables(q, d)
                toeplitz_rows(q)
                for d in range(2):
                    recur(q, d)
            dve.wait_ge(s.ysT_ready, S5_W // P)
            half = CONV // 2
            n.done(dve.memset(xraw[:, :, 0:half], 0.0))
            n.done(dve.memset(xraw[:, :, half + SEQ:], 0.0))
            for b in range(XBC // 512):
                n.wait()
                for k in range(CONV):
                    for j in range(4):
                        i = 4 * b + j
                        if k == 0:
                            dve.wait_ge(s.xbc_raw, i + 1)
                            if b >= 1:
                                dve.wait_ge(s.silu_done, i - 3)
                            r = ts(cacc[:, j], xraw[:, j, 0:SEQ], conv_w[:, i, 0:1], conv_b[:, i:i + 1], ALU.mult, ALU.add)
                        else:
                            dve.wait_ge(s.conv_tap, 16 * b + 4 * (k - 1) + j + 1)
                            r = stt(cacc[:, j], xraw[:, j, k:k + SEQ], conv_w[:, i, k:k + 1], cacc[:, j], ALU.mult, ALU.add)
                        r.then_inc(s.conv_tap if k < CONV - 1 else s.conv_done, 1)
            n.wait()
            dve.wait_ge(s.nat_copied, 16)
            dve.wait_ge(s.silu_done, 20)
            bc = lambda x: last(x, HEADDIM)
            h3 = lambda x: x.rearrange("p (h w) -> p h w", h=HG)
            n.done(dve.memset(st[:, 0, 0], 0.0))
            n.done(dve.memset(st[:, 1, TT - 1], 0.0))
            for g in range(GROUPS):
                f, b = slice(HG * g, HG * g + HG), slice(HEADS + HG * g, HEADS + HG * g + HG)
                gi = slice(GI * g, GI * g + GI)
                for j in range(TT - 1):
                    for d, c, sl in ((0, j, f), (1, TT - 1 - j, b)):
                        i = 6 * g + 2 * j + d
                        if i >= 2:
                            dve.wait_ge(s.st_ps, i - 1)
                        tt(h3(xw[:, d]), h3(xs[:, c, gi]), bc(w_end[:, c, sl]), ALU.mult).then_inc(s.xw_ready, 1)
                        nx = c + 1 if d == 0 else c - 1
                        n.wait()
                        n.link(tt(h3(st[:, d, nx]), h3(st[:, d, c]), bc(e_all[:, c, sl]), ALU.mult))
                        dve.wait_ge(s.st_ps, i + 1)
                        tt(st[:, d, nx], st[:, d, nx], ps[:, 6 + d, 0:GI], ALU.add).then_inc(s.carried, 1)
                        dve.wait_ge(s.carried, i + 1)
                for c in range(TT):
                    i = g * TT + c
                    dve.wait_ge(s.segm_exp, i + 1)
                    dve.wait_ge(s.cb_ps, i + 1)
                    n.link(tt(gmat, emat, first(ps[:, 4, 0:P], HG), ALU.mult))
                    dve.wait_ge(s.mats_ready, 2 * i + 2)
                    tt(gmat, gmat, dmat, ALU.mult).then_inc(s.g_ready, 1)
                    y0, y1, y2 = ty[:, 0], ty[:, 1], ty[:, 2]
                    dve.wait_ge(s.yd_ps, i + 1)
                    n.done(tt(h3(y0), h3(xs[:, c, gi]), bc(d_row[:, f]), ALU.mult))
                    if c >= 1:
                        n.done(tt(h3(y1), h3(ps[:, 6, 0:GI]), bc(e_cs[:, c, f]), ALU.mult))
                    if c < TT - 1:
                        n.done(tt(h3(y2), h3(ps[:, 7, 0:GI]), bc(e_cs[:, c, b]), ALU.mult))
                    n.wait()
                    for y in ([y1] if c >= 1 else []) + ([y2] if c < TT - 1 else []):
                        n.link(tt(y0, y0, y, ALU.add))
                    tt(y0, y0, ps[:, 5, 0:GI], ALU.add).then_inc(s.y_read, 1)
                    dve.wait_ge(s.y_read, i + 1)
                    dve.wait_ge(s.z_silu, g * TT + c + 1)
                    n.link(tt(ty[:, 3], y0, zg[:, g % 2, c], ALU.mult))
                    dve.tensor_tensor_reduce(out=y0, in0=ty[:, 3], in1=ty[:, 3], scale=1.0, scalar=0.0, op0=ALU.mult, op1=ALU.add,
                                             accum_out=rms[:, i % 2, 0:1]).then_inc(s.gate_ready, 1)
                    dve.wait_ge(s.rms_sqrt, i + 1)
                    n.link(dve.reciprocal(rms[:, i % 2, 2:3], rms[:, i % 2, 1:2]))
                    if i >= 1:
                        dve.wait_ge(s.yt_ps, i)
                    ts(ty[:, 4], ty[:, 3], rms[:, i % 2, 2:3], None, ALU.mult).then_inc(s.yn_ready, 1)
                    dve.wait_ge(s.yn_ready, i + 1)
            for hf in range(2):
                cs = slice(512 * hf, 512 * hf + 512)
                for c in range(TT):
                    dve.wait_ge(s.mix_ps, TT * (5 * hf + 1) + c + 1)
                    dve.wait_ge(s.mix_sig, TT * 3 * hf + c + 1)
                    tt(mix[:, c, cs], ps[:, 4 * ((5 * hf + 1) % 2) + c, :], sg_a[:, c, :], ALU.mult).then_inc(s.mix_read, 1)
                for c in range(TT):
                    dve.wait_ge(s.mix_ps, TT * (5 * hf + 4) + c + 1)
                    dve.wait_ge(s.mix_sig, TT * 3 * (hf + 1))
                    if hf or c:
                        dve.wait_ge(s.mix_ready, TT * hf + c)
                    tt(tmix, ps[:, 4 * ((5 * hf + 4) % 2) + c, :], sg_u[:, c, :], ALU.mult).then_inc(s.mix_read, 1)
                    dve.wait_ge(s.mix_read, TT * (2 * hf + 1) + c + 1)
                    n.link(tt(tmix, tmix, sg_b[:, c, :], ALU.mult))
                    tt(mix[:, c, cs], mix[:, c, cs], tmix, ALU.add).then_inc(s.mix_ready, 1)

            def norm(x, out, gb, var_sem, std_sem, c):
                for j in range(2):
                    n.done(dve.bn_stats(stats[:, j, :], x[:, 512 * j:512 * j + 512]))
                n.wait()
                dve.bn_aggr(mv[:, 0:2], stats).then_inc(var_sem, 1)
                dve.wait_ge(std_sem, c + 1)
                n.link(dve.reciprocal(mv[:, 3:4], mv[:, 2:3]))
                n.link(ts(out, x, mv[:, 0:1], mv[:, 3:4], ALU.subtract, ALU.mult))
                n.link(tt(out, out, gb[:, 0, :], ALU.mult))
                return tt(out, out, gb[:, 1, :], ALU.add)

            dve.wait_ge(s.xres_loaded, 16)
            dve.wait_ge(s.ln_loaded, 32)
            for c in range(TT):
                for j in range(2):
                    dve.wait_ge(s.wo_ps, 2 * c + j + 1)
                    r = stt(x_res[:, c, 512 * j:512 * j + 512], x_res[:, c, 512 * j:512 * j + 512], ALPHA,
                            ps[:, 2 + 2 * (c % 2) + j, :], ALU.mult, ALU.add)
                    r.then_inc(s.wo_read, 1)
                dve.wait_ge(s.wo_read, 2 * c + 2)
                norm(x_res[:, c, :], h[:, c, :], lnrow, s.var_ready, s.std_ready, c).then_inc(s.h_ready, 1)
            dve.wait_ge(s.logit_ps, 1)
            lg = ps[:, 2, 0:TT * EXPERTS].rearrange("p (c e) -> p c e", c=TT)
            n.done(dve.tensor_copy(logit, lg))
            n.link(dve.tensor_reduce(sm[:, 0, :], lg, AX.X, ALU.max))
            ts(sm[:, 1, :], sm[:, 0, :], -1.0, None, ALU.mult).then_inc(s.max_ready, 1)
            dve.wait_ge(s.rexp_done, 1)
            n.link(dve.reciprocal(sm[:, 3, :], sm[:, 2, :]))
            tt(aff, ex_t, last(sm[:, 3, :], EXPERTS), ALU.mult).then_inc(s.aff_ready, 1)
            dve.wait_ge(s.affT_copied, 1)
            for r in range(CAP // 8):
                src = affT if r == 0 else work
                n.link(dve.max(top8[:, r, :], src))
                n.link(dve.match_replace(work, top8[:, r, :], src, -1.0))
            n.link(tt(affT, affT, work, ALU.not_equal))
            n.link(dve.tensor_tensor_scan(work, affT, affT, 0.0, ALU.add, ALU.bypass))
            n.link(tt(cum, work, affT, ALU.mult))
            n.link(ts(cum, cum, -1.0, None, ALU.add))
            dve.memset(mv[:, 7:8], 0.0).then_inc(s.slotT_ready, 1)
            dve.wait_ge(s.slots_ready, 1)
            ts(acc, h, ALPHA, None, ALU.mult).then_inc(s.acc_init, 1)
            dve.wait_ge(s.acc_init, 1)
            with dve.Fori(0, EXPERTS // 4) as it:
                for u in range(2):
                    pair = 2 * it + u
                    e0 = bass.ds(4 * it + 2 * u, 2)
                    numbers = slot_no.unsqueeze(1).unsqueeze(1).to_broadcast([P, TT, 2, CAP])
                    tt(sel, numbers, last(slotv[:, :, e0], CAP), ALU.is_equal).then_inc(s.sel_built, 1)
                    dve.wait_ge(s.sel_built, pair + 1)
                    tt(selg, sel, last(aff[:, :, e0], CAP), ALU.mult).then_inc(s.sel_ready, 1)
                    for c in range(NCH):
                        i = NCH * u + c
                        dve.wait_ge(s.silu_pair, 2 * NCH * it + i + 1)
                        if i >= 2:
                            dve.wait_ge(s.hidT_ps, 2 * NCH * it + i - 1)
                        tt(hid[:, i % 2, :], s_h1[:, i % 2, :], ps[:, i % 2, 256:512], ALU.mult).then_inc(s.hid_ready, 1)
                    for k in range(2 * TT):
                        c, j = divmod(k, 2)
                        o = acc[:, c, 512 * j:512 * j + 512]
                        dve.wait_ge(s.sc_ps, 2 * TT * pair + k + 1)
                        tt(o, o, ps[:, 5 + k % 2, :], ALU.add).then_inc(s.acc_added, 1)
                    dve.wait_ge(s.acc_added, 2 * TT * pair + 2 * TT)
            dve.wait_ge(s.ln_loaded, 64)
            for c in range(TT):
                if c >= 2:
                    dve.wait_ge(out_stored[c % 2], 16 * (c // 2))
                norm(acc[:, c, :], lnout if c % 2 else lnout2, lnrow, s.ln2_var, s.ln2_std, c).then_inc(s.ln2_ready, 1)


NAMES = ["x", "w_in", "conv_w", "conv_b", "ssd_a_log_f", "ssd_a_log_b", "ssd_dt_bias_f", "ssd_dt_bias_b", "ssd_d",
         "ssd_norm_g", "w_out_ssd", "s5_a_re_f", "s5_a_im_f", "s5_log_step_f", "s5_a_re_b", "s5_a_im_b", "s5_log_step_b",
         "s5_b_re", "s5_b_im", "s5_c_re", "s5_c_im", "s5_d", "w_glu_a", "w_glu_b", "w_o", "ln1_g", "ln1_b", "w_router",
         "w_e1", "w_e3", "w_e2", "ln2_g", "ln2_b"]


def kernel(**inputs):
    import concourse.bacc as bacc
    from concourse.bass_utils import run_bass_kernel_spmd

    nc = bacc.Bacc("TRN2", target_bir_lowering=False, num_devices=1)
    arrays = {f"in_{n}": np.ascontiguousarray(inputs[n]) for n in NAMES}
    aps = {n: nc.dram_tensor(f"in_{n}", arrays[f"in_{n}"].shape, F32, kind="ExternalInput").ap() for n in NAMES}
    out = nc.dram_tensor("out", (1, SEQ, D_MODEL), F32, kind="ExternalOutput").ap()
    encoder(nc, aps, out)
    return run_bass_kernel_spmd(nc, [arrays], core_ids=[0]).results[0]["out"]
```

```python
from contextlib import ExitStack

import numpy as np
import concourse.bass as bass
from concourse import mybir

F32 = mybir.dt.float32
ALU = mybir.AluOpType
ACT = mybir.ActivationFunctionType
AX = mybir.AxisListType

P = 128
D_MODEL, SEQ = 1024, 512
KT = D_MODEL // P
TT = SEQ // P
HEADS, HEADDIM, GROUPS = 24, 64, 4
HG = HEADS // GROUPS
GI = HG * HEADDIM
INNER = HEADS * HEADDIM
XBC = INNER + 2 * GROUPS * P
CONV = 5
S5_W, S5_K, S5_P = 768, 16, 64
S5_G = S5_W // S5_K
GP = S5_G // 2
T = 4
NC = SEQ // T
PARAMS = 22
QB = 4
NQ = GP // QB
COL_Z, COL_XBC = 0, INNER
COL_DT = COL_XBC + XBC
COL_U = COL_DT + 2 * HEADS
COL_GA = COL_U + S5_W
COL_GB = COL_GA + D_MODEL
EXPERTS, FF = 16, 2816
CAP = 2 * SEQ // EXPERTS
FC = 256
NCH = FF // FC
U_SLICES = (0, 1, 4, 6)
ALPHA = 2.0 ** 0.25
EPS = 1e-5

TWO_PI = 2 * np.pi
PI_1 = 6.28125
PI_2 = float(np.float32(np.floor((TWO_PI - PI_1) * 2 ** 22) / 2 ** 22))
PI_3 = float(np.float32(TWO_PI - PI_1 - PI_2))
ROUND = 12582912.0
PI_LIM = 3.1415925


class Space:

    def __init__(self, arena, at, end):
        self.arena, self.at, self.end = arena, at, end

    def take(self, *shape, parts=P):
        n = int(np.prod(shape))
        v = self.arena[0:parts, self.at:self.at + n]
        self.at += n
        assert self.at <= self.end, (self.at, self.end)
        if len(shape) > 1:
            names = "abcdef"[:len(shape)]
            v = v.rearrange(f"p ({' '.join(names)}) -> p {' '.join(names)}", **dict(zip(names, shape)))
        return v


class Steps:

    def __init__(self, eng, sem):
        self.eng, self.sem, self.n = eng, sem, 0

    def done(self, ins):
        ins.then_inc(self.sem, 1)
        self.n += 1
        return ins

    def wait(self):
        self.eng.wait_ge(self.sem, self.n)

    def link(self, ins):
        self.done(ins)
        self.wait()


def last(ap, n):
    s = list(ap.shape)
    return ap.unsqueeze(len(s)).to_broadcast(s + [n])


def mid2(ap, n):
    return ap.unsqueeze(2).to_broadcast([ap.shape[0], ap.shape[1], n, ap.shape[2]])


def first(ap, n):
    return ap.unsqueeze(1).to_broadcast([ap.shape[0], n, ap.shape[1]])


def weight_slices():
    s = [("w_in", 0, KT, COL_U + P * U_SLICES[i], P * (U_SLICES[i + 1] - U_SLICES[i])) for i in range(3)]
    s += [("w_in", 0, KT, COL_DT, 2 * HEADS)]
    s += [("w_in", 0, KT, c0 + 512 * n, 512) for n in range(2) for c0 in (COL_GA, COL_GB)]
    s += [("w_in", 0, KT, COL_XBC + 512 * i, 512) for i in range(XBC // 512)]
    s += [("w_in", 0, KT, COL_Z + GI * g, GI) for g in range(GROUPS)]
    for n in range(2):
        s += [("glu_b", 0, 6, 512 * n, 512), ("glu_a", 0, 6, 512 * n, 512),
              ("w_out", 0, 6, 512 * n, 512), ("w_out", 6, 6, 512 * n, 512)]
    s += [("w_o", 0, KT, 0, 512), ("w_o", 0, KT, 512, 512)]
    return s


def encoder(nc, A, out):
    SL = weight_slices()
    FIRST_GATE = 4
    FIRST_XBC = FIRST_GATE + 4
    FIRST_Z = FIRST_XBC + XBC // 512
    GATES = 4 * TT
    EARLY = 2
    gates_before = [EARLY] + [min(GATES, EARLY + 4 + 2 * q) for q in range(NQ)]
    FIRST_MIX = FIRST_Z + GROUPS
    NW = 2
    w_dram = {"w_in": A["w_in"][0], "w_out": A["w_out_ssd"][0], "glu_a": A["w_glu_a"][0],
              "glu_b": A["w_glu_b"][0], "w_o": A["w_o"][0]}
    u_dram = nc.dram_tensor("u_scratch", (S5_W, T, NC), F32, kind="Internal").ap()
    y_dram = nc.dram_tensor("y_scratch", (S5_W, T, NC), F32, kind="Internal").ap()
    g_dram = nc.dram_tensor("gate_scratch", (4, P, TT, 512), F32, kind="Internal").ap()
    toep_dram = nc.dram_tensor("toeplitz_scratch", (S5_W, (2 * T - 1) * S5_K), F32, kind="Internal").ap()

    with ExitStack() as ctx:
        WORDS = 53200
        arena = ctx.enter_context(nc.sbuf_tensor("arena", [P, WORDS], F32))
        ps = ctx.enter_context(nc.psum_tensor("ps", [P, 8, 512], F32))

        def sem(name):
            return ctx.enter_context(nc.semaphore(name))

        C = Space(arena, 0, 2300)
        ident, m_le, m_gt, m_ge, m_lt, ones = (C.take(P) for _ in range(6))
        chunk_no = C.take(NC)
        slot_no = C.take(CAP)
        eps_col = C.take(1)
        conv_w, conv_b = C.take(XBC // P, CONV), C.take(XBC // P)
        dt_bias, a_neg = C.take(2 * HEADS), C.take(2 * HEADS)
        d_row, norm_g = C.take(HEADS), C.take(INNER // P)
        dtime = C.take(TT, 2 * HEADS)
        da, w_end, e_cs, e_all = (C.take(TT, 2 * HEADS) for _ in range(4))
        C0 = C.at
        W0 = WORDS - NW * KT * 512
        wring = Space(arena, W0, WORDS).take(NW, KT, 512)

        R = Space(arena, C0, W0)
        xT = R.take(KT, SEQ)
        ysT = R.take(S5_W // P, SEQ)
        yT_at = R.at
        uT = ysT
        S = Space(arena, R.at, W0)
        x_nat = S.take(TT, D_MODEL)
        vbd = x_nat.rearrange("p a b -> p (a b)").rearrange("p (n g d r c) -> p n g d r c", n=2, g=QB, d=2, r=2)
        U = S.take(GP, NC)
        M = S.take(GP, P)
        vc = S.take(2, QB, 2, 2, (T + 1) * S5_K)
        wc = S.take(QB, 2, 2, T * S5_K)
        wbd = S.take(QB, 2, 2, P)
        wT = S.take(2, 4, P)
        bbar = S.take(2, 2, GP, S5_K)
        c_map = S.take(2, GP, S5_K)
        bpad = S.take(QB, 2, 2, 2 * S5_K)
        par = S.take(2, 3, GP)
        small = S.take(31, 2, GP)
        pt = S.take(2, 2, 2, GP, T + 1)
        toep = S.take(QB, 2 * T - 1, S5_K, parts=2 * S5_K)
        eye2, d_diag, d_col = S.take(S5_K, parts=32), S.take(GP, S5_K, parts=32), S.take(GP, parts=32)
        LEVELS = 7
        rot = S.take(2, LEVELS, 2, GP)
        pool_tmp = S.take(4, QB * 64)
        cos_t, sin_t = S.take(2, QB, NC), S.take(2, QB, NC)
        zr, zi, t1, t2, sr, si = (S.take(QB, NC) for _ in range(6))
        E = Space(arena, S.at, W0)
        b_raw, c_nat = E.take(2, GP, S5_K), E.take(GP // 8, 2, P)
        par_raw = E.take(6, P, parts=GP)
        ls_raw = E.take(2, 2, parts=GP)
        vec_a, vec_b, vec_d = E.take(P, parts=120), E.take(P, parts=INNER // P), E.take(2 * S5_K, parts=GP)
        rot_flat = [rot[:, r].rearrange("p l d g -> p (l d g)") for r in range(2)]
        X = S.take(2, 2, 2, QB, NC)
        y5 = S.take(QB * NC)
        gstage = S.take(512)
        ang, ang_half = y5[:, 0:LEVELS * 2 * GP], gstage[:, 0:LEVELS * 2 * GP]

        Z_AHEAD = 2
        S = Space(arena, yT_at, W0)
        yT = S.take(INNER // P, SEQ)
        mix_at = S.at
        xs = S.take(TT, INNER)
        bn = S.take(TT, GROUPS * P)
        bT, cT = S.take(GROUPS, SEQ), S.take(GROUPS, SEQ)
        zg_odd, zg_even = S.take(TT, GI), S.take(TT, GI)
        zg = (zg_even, zg_odd)
        ty5 = Space(arena, S.at - TT * GI, W0).take(S5_W // P, SEQ)
        st = S.take(2, 2, TT - 1, GI)
        xw = S.take(2, GI)
        ty = S.take(5, GI)
        rms = S.take(2, 4)
        S2 = Space(arena, S.at, W0)
        xraw = S2.take(4, SEQ + CONV - 1)
        cacc = S2.take(4, SEQ)
        xc = S2.take(4, SEQ)
        S = Space(arena, S.at, W0)
        dmat, uf, emat, gmat = S.take(HG, P), S.take(HG, P), S.take(HG, P), S.take(2, HG, P)
        S = Space(arena, S2.at - 4 * SEQ, W0)
        rhs_f, rhs_b = S.take(HG, P), S.take(HG, P)

        S = Space(arena, mix_at, W0)
        sg = S.take(2, 2, TT, 512)
        sg_u = S.take(TT, 512)
        tmix = S.take(512)
        RING = 12 * 2048
        S = Space(arena, max(S.at, C0 + RING), W0)
        mix = S.take(TT, D_MODEL)
        mixT = S.take(2, KT, P)
        mix_end = S.at
        x_res = S.take(TT, D_MODEL)
        h = S.take(TT, D_MODEL)
        lnrow = S.take(2, D_MODEL)
        stats, mv = S.take(2, 6), S.take(TT, 4)
        w_r = S.take(KT, EXPERTS)
        hT = S.take(KT, P)
        m_bank = ((0, 2, 3, 4), (1, 5, 6, 7))
        o_bank = ((3, 4), (6, 7))
        acc = x_res
        S3 = Space(arena, W0, WORDS)
        logit, ex_t = S3.take(TT, EXPERTS), S3.take(TT, EXPERTS)
        sm = S3.take(4, TT)
        affT, work, cum = (S3.take(SEQ, parts=EXPERTS) for _ in range(3))
        top8 = S3.take(CAP // 8, 8, parts=EXPERTS)
        ring = arena[:, C0:C0 + RING].rearrange("p (k n w) -> p k n w", k=6, n=2)
        S = Space(arena, C0 + RING, mix_end)
        aff, slotv = S.take(TT, EXPERTS), S.take(TT, EXPERTS)
        sel, selg = S.take(TT, 2, CAP), S.take(TT, 2, CAP)
        selgT = S.take(TT, P)
        xin = S.take(KT, P)
        s_h1, hid, hidT = S.take(2, 256), S.take(2, 256), S.take(2, 2, P)
        ye = S.take(D_MODEL)

        names = """b_loaded params_loaded broadcasts_loaded consts_ready xT_ps xT_copied vec_ps u_ps u_copied u_stored u_loaded
        dt_ps dt_abs dt_exp dt_ln da_ready seg_ps seg_exp ls_filled step_exp lr_ready tanh_done theta_ready
        sin_done v_ready w_ready rot_angle rot_sin rot_ready gate_ps gate_copied g_stored sg_loaded bd_ready
        toep_ps toep_built toep_stored toep_loaded wT_ps wT_copied F_ps F_read par_ready conv_tap sel_built
        tab_ready X_ready y5_ps y5_copied y5_stored yT5_loaded ysT_ready slice_used dve_step act_step
        pool_step m_cleared maps_cleared xbc_ps xbc_raw conv_done silu_done nat_ps nat_copied z_ps z_silu
        xw_ready st_ps carried cb_ps segm_ps segm_exp mats_ready g_ready yd_ps y_read gate_ready rms_sqrt
        yn_ready yt_ps yt_copied mix_ps mix_sig mix_read glu_done mix_ready mixT_ps mixT_copied wo_ps wo_read
        var_ready std_ready h_ready xres_loaded ln_loaded hT_ps hT_copied wr_loaded logit_ps max_ready
        rexp_done aff_ready affT_ps affT_copied slotT_ready slot_ps slots_ready sel_ready xin_ps xin_copied
        selT_ps selT_copied silu_pair hid_ready hidT_ps hidT_copied ye_copied sc_ps acc_added acc_init ln2_var
        ln2_std ln2_ready out_stored""".split()
        sems = {n: sem(n) for n in names}
        x_loaded = [sem(f"x_loaded_{i}") for i in range(TT)]
        slice_loaded = [sem(f"slice_loaded_{i}") for i in range(NW)]
        w_loaded = [[sem(f"expert_{k}_{i}_loaded") for i in range(2)] for k in range(6)]
        w_used = [sem(f"expert_{k}_used") for k in range(6)]
        s = type("Sems", (), sems)

        w_rows = {n: w_dram[n] for n in w_dram}
        block = ctx.enter_context(nc.Block())

        @block.sync
        def _(sp):
            for c in range(TT):
                sp.dma_start(x_nat[:, c], A["x"][0][P * c:P * c + P]).then_inc(x_loaded[c], 16)

            def released(i):
                if i < FIRST_GATE:
                    return (s.u_ps, U_SLICES[i + 1]) if i < 3 else (s.dt_ps, 1)
                if i < FIRST_XBC:
                    return s.gate_ps, TT * (i - FIRST_GATE + 1)
                if i < FIRST_Z:
                    return s.xbc_ps, 4 * (i - FIRST_XBC + 1)
                if i < FIRST_MIX:
                    return s.z_ps, TT * (i - FIRST_Z + 1)
                half, j = divmod(i - FIRST_MIX, 4)
                if j == 2:
                    return s.slice_used, half + 1
                return s.mix_ps, TT * (3 * half + min(j + 1, 3))

            def slices(i0, i1):
                for i in range(i0, i1):
                    name, k0, nk, c0, w = SL[i]
                    if i >= NW:
                        sp.wait_ge(*released(i - NW))
                    src = w_rows[name].rearrange("(k p) n -> p k n", p=P)[:, k0:k0 + nk, c0:c0 + w]
                    sp.dma_start(wring[:, i % NW, 0:nk, 0:w], src).then_inc(slice_loaded[i % NW], 16)

            def toeplitz_blocks(q):
                sp.wait_ge(s.toep_built, q + 1)
                sp.dma_start(toep_dram.rearrange("(g j) w -> j g w", j=2 * S5_K)[:, QB * q:QB * q + QB, :],
                             toep.rearrange("p g i k -> p g (i k)")).then_inc(s.toep_stored, 16)
                sp.wait_ge(s.toep_stored, 16 * (q + 1))
                for b in range(2):
                    for t in range(T):
                        r0 = b * T * S5_K + t * S5_K
                        src = toep_dram.rearrange("(g b j) w -> b j g w", b=2, j=S5_K)[
                            b, :, QB * q:QB * q + QB, (T - 1 - t) * S5_K:(2 * T - 1 - t) * S5_K]
                        sp.dma_start(M[r0:r0 + S5_K, QB * q:QB * q + QB, b * T * S5_K:(b + 1) * T * S5_K], src).then_inc(s.toep_loaded, 16)

            def y_to_dram(q):
                sp.wait_ge(s.y5_copied, q + 1)
                for b in range(2):
                    for t in range(T):
                        r0 = b * T * S5_K + t * S5_K
                        dst = y_dram.rearrange("(g b k) t c -> b t k g c", b=2, k=S5_K)[b, t, :, QB * q:QB * q + QB, :]
                        sp.dma_start(dst, y5[r0:r0 + S5_K].rearrange("p (g c) -> p g c", g=QB)).then_inc(s.y5_stored, 16)

            slices(0, FIRST_GATE + 1)
            sp.wait_ge(s.u_stored, 16 * (S5_W // P))
            for b in range(2):
                for t in range(T):
                    r0 = b * T * S5_K + t * S5_K
                    sp.dma_start(U[r0:r0 + S5_K], u_dram.rearrange("(g b j) s c -> b s j g c", b=2, j=S5_K)[b, t]).then_inc(s.u_loaded, 16)
            slices(FIRST_GATE + 1, FIRST_GATE + 2)
            sp.wait_ge(s.m_cleared, 1)
            i = FIRST_GATE + 2
            for q in range(NQ):
                toeplitz_blocks(q)
                if q >= 1:
                    y_to_dram(q - 1)
                while i < FIRST_XBC + 2 and gates_before[q + 1] >= TT * (i - 1 - FIRST_GATE):
                    slices(i, i + 1)
                    i += 1
            y_to_dram(NQ - 1)
            slices(FIRST_XBC + 2, FIRST_MIX + 1)
            sp.wait_ge(s.gate_ready, (GROUPS - 1) * TT)
            sp.wait_ge(s.y5_stored, 16 * 2 * T * NQ)
            sp.dma_start(ty5, y_dram.rearrange("(n p) t c -> p n (t c)", p=P)).then_inc(s.yT5_loaded, 16)
            slices(FIRST_MIX + 1, FIRST_MIX + 2)
            sp.wait_ge(s.yt_copied, 3 * GROUPS * TT)
            sp.wait_ge(s.g_stored, 16 * GATES)
            for half in range(2):
                for j in range(2):
                    sp.dma_start(sg[:, half, j], g_dram[2 * half + j]).then_inc(s.sg_loaded, 16)
            slices(FIRST_MIX + 2, len(SL))
            sp.wait_ge(s.mix_ps, 1)
            sp.dma_start(x_res, A["x"][0].rearrange("(t p) d -> p t d", p=P)).then_inc(s.xres_loaded, 16)
            for i, name in enumerate(("ln1_g", "ln1_b")):
                sp.dma_start(lnrow[:, i, :], A[name][0].partition_broadcast(P)).then_inc(s.ln_loaded, 16)
            sp.dma_start(w_r, A["w_router"][0].rearrange("(k p) e -> p k e", p=P)).then_inc(s.wr_loaded, 16)
            w_e = [A["w_e1"][0], A["w_e3"][0], A["w_e2"][0]]
            with sp.Fori(0, EXPERTS // 4) as it:
                for u in range(2):
                    for c in range(NCH):
                        i = NCH * u + c
                        for kind in range(6):
                            which, e = divmod(kind, 2)
                            w = w_e[which][bass.ds(4 * it + 2 * u + e, 1)].rearrange("a m n -> (a m) n")
                            if which < 2:
                                src = w.rearrange("(k p) f -> p k f", p=P)[:, :, FC * c:FC * c + FC]
                                dst = ring[:, kind, i % 2].rearrange("p (k f) -> p k f", k=KT)
                            else:
                                src = w[FC * c:FC * c + FC].rearrange("(j p) d -> p j d", p=P)
                                dst = ring[:, kind, i % 2].rearrange("p (j d) -> p j d", j=2)
                            sp.wait_ge(w_used[kind], 2 * NCH * it + i + 1)
                            sp.dma_start(dst, src).then_inc(w_loaded[kind][i % 2], 16)
            for c in range(TT):
                sp.wait_ge(s.ln2_ready, c + 1)
                sp.dma_start(out[0][P * c:P * c + P], acc[:, c, :]).then_inc(s.out_stored, 16)
            sp.wait_ge(s.out_stored, 16 * TT)

        def state_maps(eng, n, tmp, q):
            if q >= 1:
                eng.wait_ge(s.bd_ready, q)
            gs = slice(QB * q, QB * q + QB)
            tmp = [x.rearrange("p (g i k) -> p g i k", g=QB, k=S5_K) for x in tmp]
            for d in range(2):
                powers = pt[:, 1, :, 0, gs, 1:] if d == 0 else pt[:, 0, :, 1, gs, 0:T]
                b_re, b_im = (mid2(bbar[:, d, r, gs, :], T) for r in range(2))
                p_re, p_im = (last(powers[:, r], S5_K) for r in range(2))
                o = [wc[:, :, d, r, :].rearrange("p g (i k) -> p g i k", k=S5_K) for r in range(2)]
                for t, (x, y) in enumerate(((p_re, b_re), (p_im, b_im), (p_re, b_im), (p_im, b_re))):
                    n.done(eng.tensor_tensor(tmp[t], x, y, ALU.mult))
                n.wait()
                n.done(eng.tensor_tensor(o[0], tmp[0], tmp[1], ALU.subtract))
                ins = eng.tensor_tensor(o[1], tmp[2], tmp[3], ALU.add)
                if d == 0:
                    n.link(ins)
                else:
                    ins.then_inc(s.w_ready, 1)
                    eng.wait_ge(s.w_ready, q + 1)
                    n.wait()

        @block.gpsimd
        def _(pool):
            n = Steps(pool, s.pool_step)
            n.link(pool.memset(ones, 1.0))
            pool.memset(eps_col, EPS).then_inc(s.consts_ready, 1)
            for m, step, op in ((ident, 1, ALU.is_equal), (m_le, 1, ALU.is_ge), (m_gt, -1, ALU.is_gt), (m_ge, -1, ALU.is_ge), (m_lt, 1, ALU.is_gt)):
                pool.affine_select(out=m, in_=ones, pattern=[[step, P]], compare_op=op, fill=0.0, base=0,
                                   channel_multiplier=-step).then_inc(s.consts_ready, 1)
            pool.iota(chunk_no, pattern=[[1, NC]], base=0, channel_multiplier=0,
                      allow_small_or_imprecise_dtypes=True).then_inc(s.consts_ready, 1)
            pool.iota(slot_no, pattern=[[1, CAP]], base=1, channel_multiplier=0,
                      allow_small_or_imprecise_dtypes=True).then_inc(s.consts_ready, 1)
            pool.memset(bpad, 0.0).then_inc(s.maps_cleared, 1)
            pool.memset(wbd, 0.0).then_inc(s.maps_cleared, 1)
            pool.memset(M, 0.0).then_inc(s.m_cleared, 1)
            pool.wait_ge(s.xT_ps, KT)
            pool.memset(vbd, 0.0).then_inc(s.maps_cleared, 1)

            def tables(q, d):
                gs = slice(QB * q, QB * q + QB)
                if q >= 1:
                    pool.wait_ge(s.X_ready, 2 * (q - 1) + d + 1)
                c, sn = cos_t[:, d], sin_t[:, d]
                n.done(pool.memset(c[:, :, 0:1], 1.0))
                n.link(pool.memset(sn[:, :, 0:1], 0.0))
                for k in range(LEVELS):
                    m = 2 ** k
                    re, im = (last(rot[:, r, k, d, gs], m) for r in range(2))
                    tmp = [pool_tmp[:, i, 0:QB * m].rearrange("p (g c) -> p g c", g=QB) for i in range(4)]
                    for t, (x, y) in enumerate(((c, re), (sn, im), (c, im), (sn, re))):
                        n.done(pool.tensor_tensor(tmp[t], x[:, :, 0:m], y, ALU.mult))
                    n.wait()
                    n.done(pool.tensor_tensor(c[:, :, m:2 * m], tmp[0], tmp[1], ALU.subtract))
                    ins = pool.tensor_tensor(sn[:, :, m:2 * m], tmp[2], tmp[3], ALU.add)
                    if k < LEVELS - 1:
                        n.link(ins)
                    else:
                        ins.then_inc(s.tab_ready, 1)
                        n.wait()

            pool.wait_ge(s.rot_ready, 1)
            for q in range(NQ):
                for d in range(2):
                    tables(q, d)
                    pool.wait_ge(s.tab_ready, 2 * q + d + 1)
            pool.wait_ge(s.nat_ps, 12)
            for i in range(GROUPS * TT):
                g, c = divmod(i, TT)
                f, b = slice(HG * g, HG * g + HG), slice(HEADS + HG * g, HEADS + HG * g + HG)
                if i >= 1:
                    pool.wait_ge(s.mats_ready, 2 * i)
                    pool.wait_ge(s.segm_ps, i)
                pool.tensor_tensor(rhs_f, first(m_le, HG), last(da[:, c, f], P), ALU.mult)
                pool.tensor_tensor(rhs_b, first(m_ge, HG), last(da[:, c, b], P), ALU.mult).then_inc(s.mats_ready, 1)
                if i == 0:
                    pool.wait_ge(s.silu_done, 20)
                if i >= 1:
                    pool.wait_ge(s.g_ready, i)
                pool.tensor_tensor(uf, first(m_le, HG), last(dtime[:, c, f], P), ALU.mult)
                n.link(pool.tensor_tensor(dmat, first(m_ge, HG), last(dtime[:, c, b], P), ALU.mult))
                pool.tensor_tensor(dmat, dmat, uf, ALU.add).then_inc(s.mats_ready, 1)

        @block.scalar
        def _(act):
            n = Steps(act, s.act_step)

            def f(out, in_, func, **kw):
                return act.activation(out, in_, func, **kw)

            for d, side in enumerate("fb"):
                act.dma_start(par_raw[:, 3 * d, :], A["s5_a_re_" + side][0].rearrange("(g b) p -> g (b p)", b=2)).then_inc(s.params_loaded, 16)
                act.dma_start(par_raw[:, 3 * d + 1, :], A["s5_a_im_" + side][0].rearrange("(g b) p -> g (b p)", b=2)).then_inc(s.params_loaded, 16)
                act.dma_start(ls_raw[:, d, :], A["s5_log_step_" + side][0].rearrange("(g b) -> g b", b=2)).then_inc(s.params_loaded, 16)
            for r, name in enumerate(("s5_c_re", "s5_c_im")):
                for q in range(GP // 8):
                    for b in range(2):
                        act.dma_start(c_nat[:, q, r, b * S5_P:(b + 1) * S5_P],
                                       A[name][0].rearrange("(g b) k p -> b g k p", b=2)[b, 8 * q:8 * q + 8]).then_inc(s.params_loaded, 16)
            act.dma_start(vec_a[0:100], A["conv_w"][0].rearrange("k (t p) -> (k t) p", p=P)).then_inc(s.params_loaded, 16)
            act.dma_start(vec_a[100:120], A["conv_b"][0].rearrange("(t p) -> t p", p=P)).then_inc(s.params_loaded, 16)
            act.dma_start(vec_b, A["ssd_norm_g"][0].rearrange("(t p) -> t p", p=P)).then_inc(s.params_loaded, 16)
            act.dma_start(vec_d, A["s5_d"][0].rearrange("(g j) -> g j", j=2 * S5_K)).then_inc(s.params_loaded, 16)
            for d, side in enumerate("fb"):
                c = slice(d * HEADS, (d + 1) * HEADS)
                act.dma_start(dt_bias[:, c], A["ssd_dt_bias_" + side][0].partition_broadcast(P)).then_inc(s.broadcasts_loaded, 16)
                act.dma_start(a_neg[:, c], A["ssd_a_log_" + side][0].partition_broadcast(P)).then_inc(s.broadcasts_loaded, 16)
            act.dma_start(d_row, A["ssd_d"][0].partition_broadcast(P)).then_inc(s.broadcasts_loaded, 16)
            for r, name in enumerate(("s5_b_re", "s5_b_im")):
                act.dma_start(b_raw[:, r], A[name][0].rearrange("(g b) p k -> (b p) g k", b=2)).then_inc(s.b_loaded, 16)
            act.wait_ge(s.par_ready, 1)
            f(small[:, 0], par[:, :, 2, :], ACT.Exp).then_inc(s.step_exp, 1)
            act.wait_ge(s.lr_ready, 1)
            f(small[:, 3], small[:, 1], ACT.Tanh, scale=0.5).then_inc(s.tanh_done, 1)
            act.wait_ge(s.theta_ready, 1)
            f(small[:, 5], small[:, 4], ACT.Sin)
            f(small[:, 6], small[:, 4], ACT.Sin, scale=0.5).then_inc(s.sin_done, 1)
            for c in range(S5_W // P):
                act.wait_ge(s.u_ps, c + 1)
                f(uT[:, c, :].rearrange("p (s c) -> p c s", s=T), ps[:, c % 2, :].rearrange("p (c s) -> p c s", s=T),
                  ACT.Copy).then_inc(s.u_copied, 1)
                act.wait_ge(s.u_copied, c + 1)
                act.dma_start(u_dram[P * c:P * (c + 1)], uT[:, c, :].rearrange("p (s c) -> p s c", s=T)).then_inc(s.u_stored, 16)
                if c == 3:
                    act.wait_ge(s.rot_angle, 1)
                    f(rot_flat[1], ang, ACT.Sin)
                    f(ang_half, ang, ACT.Sin, scale=0.5).then_inc(s.rot_sin, 1)
            act.wait_ge(s.dt_abs, 1)
            f(w_end[:, :, :], w_end[:, :, :], ACT.Exp, scale=-1.0).then_inc(s.dt_exp, 1)
            act.wait_ge(s.dt_exp, 1)
            f(w_end[:, :, :], w_end[:, :, :], ACT.Ln, bias=ones[:, 0:1]).then_inc(s.dt_ln, 1)
            act.wait_ge(s.broadcasts_loaded, 80)
            f(a_neg, a_neg, ACT.Exp).then_inc(s.dt_ln, 1)

            def block_diagonal(q):
                act.wait_ge(s.v_ready, q + 1)
                act.wait_ge(s.w_ready, q + 1)
                if q >= 1:
                    act.wait_ge(s.bd_ready, q)
                    act.wait_ge(s.wT_ps, QB * q)
                    act.wait_ge(s.toep_ps, q)
                if q >= 2:
                    act.wait_ge(s.y5_ps, q - 1)
                for b in range(2):
                    p, c = slice(64 * b, 64 * b + 64), slice(64 * b, 64 * b + 64)
                    for d in range(2):
                        i0 = S5_K if d == 0 else 0
                        f(vbd[p, q % 2, :, d, :, c], vc[p, q % 2, :, d, :, i0:i0 + 64], ACT.Copy)
                        f(wbd[p, :, d, :, c], wc[p, :, d, :, :], ACT.Copy)
                        r = f(bpad[p, :, d, :, S5_K * b:S5_K * b + S5_K],
                              bbar[p, d, :, QB * q:QB * q + QB, :].rearrange("p r g k -> p g r k"), ACT.Copy)
                r.then_inc(s.bd_ready, 1)

            def gate(t, bank):
                act.wait_ge(s.gate_ps, t + 1)
                if t >= 1:
                    act.wait_ge(s.g_stored, 16 * t)
                f(gstage, ps[:, bank, :], ACT.Sigmoid).then_inc(s.gate_copied, 1)
                act.wait_ge(s.gate_copied, t + 1)
                act.dma_start(g_dram[t // TT, :, t % TT, :], gstage).then_inc(s.g_stored, 16)

            act.wait_ge(s.maps_cleared, 3)
            block_diagonal(0)
            for t in range(EARLY):
                gate(t, t % 2)
            act.wait_ge(s.seg_ps, 1)
            H = HEADS
            seg = ps[:, 5, 0:16 * H].rearrange("p (k c h) -> p k c h", k=4, c=TT)
            f(e_cs[:, :, 0:H], seg[:, 0], ACT.Exp)
            f(e_cs[:, :, H:2 * H], seg[:, 1], ACT.Exp)
            f(w_end[:, :, 0:H], seg[:, 2], ACT.Exp)
            f(w_end[:, :, H:2 * H], seg[:, 3], ACT.Exp)
            f(e_all, ps[:, 6, 0:8 * H].rearrange("p (c h) -> p c h", c=TT), ACT.Exp).then_inc(s.seg_exp, 1)

            def gelu(q):
                act.wait_ge(s.y5_ps, q + 1)
                if q >= 1:
                    act.wait_ge(s.y5_stored, 16 * 2 * T * q)
                f(y5, ps[:, 7, :], ACT.Gelu_apprx_tanh).then_inc(s.y5_copied, 1)

            for q in range(NQ):
                for j in range(QB):
                    i = QB * q + j
                    act.wait_ge(s.wT_ps, i + 1)
                    if i >= 2:
                        act.wait_ge(s.F_ps, i - 1)
                    f(wT[:, i % 2].rearrange("p a b -> p (a b)"), ps[:, 5 + i % 2, :], ACT.Copy).then_inc(s.wT_copied, 1)
                if q >= 1:
                    gelu(q - 1)
                if q + 1 < NQ:
                    block_diagonal(q + 1)
                for t in range(gates_before[q], gates_before[q + 1]):
                    gate(t, (4, 7)[t % 2])
            gelu(NQ - 1)
            for b in range(XBC // 512 + 1):
                for j in range(4):
                    i = 4 * b + j
                    if i < 20:
                        act.wait_ge(s.xbc_ps, i + 1)
                        if b >= 1:
                            act.wait_ge(s.conv_done, 4 * b)
                        f(xraw[:, j, 2:2 + SEQ], ps[:, i % 2, :], ACT.Copy).then_inc(s.xbc_raw, 1)
                for j in range(4):
                    i = 4 * (b - 1) + j
                    if 0 <= i < 16:
                        act.wait_ge(s.nat_ps, i + 1)
                        src = ps[:, 2 + i % 2, :].rearrange("p (c w) -> p c w", c=TT)
                        dst = xs[:, :, P * i:P * i + P] if i < 12 else bn[:, :, P * (i - 12):P * (i - 11)]
                        f(dst, src, ACT.Copy).then_inc(s.nat_copied, 1)
                for j in range(4):
                    i = 4 * b + j
                    if i < 20:
                        if i == 0:
                            act.wait_ge(s.y5_stored, 16 * 2 * T * NQ)
                            act.wait_ge(s.g_stored, 16 * GATES)
                        act.wait_ge(s.conv_done, i + 1)
                        if 4 <= i < 12:
                            act.wait_ge(s.nat_ps, i - 3)
                        dst = xc[:, j, :] if i < 12 else (bT[:, i - 12, :] if i < 16 else cT[:, i - 16, :])
                        f(dst, cacc[:, j, :], ACT.Silu).then_inc(s.silu_done, 1)

            def z_gate(g, c):
                act.wait_ge(s.z_ps, g * TT + c + 1)
                if g >= 2 and c == 0:
                    act.wait_ge(s.gate_ready, (g - 1) * TT)
                f(zg[g % 2][:, c, :], ps[:, int(g * TT + c == 1), 0:GI], ACT.Silu).then_inc(s.z_silu, 1)

            def decays(i):
                act.wait_ge(s.segm_ps, i + 1)
                if i >= 1:
                    act.wait_ge(s.g_ready, i)
                f(emat.rearrange("p (a b) q -> p a (b q)", a=2), ps[:, 2:4, 0:GI], ACT.Exp).then_inc(s.segm_exp, 1)

            def y_copied(i):
                g, c = divmod(i, TT)
                act.wait_ge(s.yt_ps, i + 1)
                for j in range(3):
                    f(yT[:, 3 * g + j, P * c:P * c + P], ps[:, 1, P * j:P * (j + 1)], ACT.Copy,
                      scale=norm_g[:, 3 * g + j:3 * g + j + 1]).then_inc(s.yt_copied, 1)

            z_gate(0, 0)
            decays(0)
            for c in range(1, Z_AHEAD):
                z_gate(0, c)
            for i in range(GROUPS * TT):
                g, c = divmod(i, TT)
                if i + 1 < GROUPS * TT:
                    decays(i + 1)
                if i >= 1:
                    y_copied(i - 1)
                act.wait_ge(s.gate_ready, i + 1)
                f(rms[:, i % 2, 1:2], rms[:, i % 2, 0:1], ACT.Sqrt, scale=1.0 / GI, bias=eps_col).then_inc(s.rms_sqrt, 1)
                if i + Z_AHEAD < GROUPS * TT:
                    z_gate(*divmod(i + Z_AHEAD, TT))
                elif c == TT - 2:
                    act.wait_ge(s.yT5_loaded, 16)
                    for k in range(S5_W // P):
                        f(ysT[:, k, :].rearrange("p (c s) -> p c s", s=T), ty5[:, k, :].rearrange("p (s c) -> p c s", s=T),
                          ACT.Copy).then_inc(s.ysT_ready, 1)
            y_copied(GROUPS * TT - 1)
            for half in range(2):
                m = 3 * half
                for c in range(TT):
                    act.wait_ge(s.mix_ps, TT * m + c + 1)
                    if half:
                        act.wait_ge(s.mix_read, TT)
                        act.wait_ge(s.glu_done, TT)
                    f(sg_u[:, c, :], ps[:, m_bank[m % 2][c], :], ACT.Sigmoid).then_inc(s.mix_sig, 1)

            def mix_transposed(c):
                for j in range(2):
                    act.wait_ge(s.mixT_ps, 2 * c + j + 1)
                    if c >= 2:
                        act.wait_ge(s.wo_ps, 2 * (c - 1))
                    f(mixT[:, c % 2, 4 * j:4 * j + 4, :].rearrange("p a b -> p (a b)"), ps[:, 2 * j, :], ACT.Copy).then_inc(s.mixT_copied, 1)

            def deviation(c):
                act.wait_ge(s.var_ready, c + 1)
                f(mv[:, c, 2:3], mv[:, c, 1:2], ACT.Sqrt, bias=eps_col).then_inc(s.std_ready, 1)

            def h_transposed(c):
                for j in range(2):
                    act.wait_ge(s.hT_ps, 2 * c + j + 1)
                    if c >= 1:
                        act.wait_ge(s.logit_ps, c)
                    f(hT[:, 4 * j:4 * j + 4, :].rearrange("p a b -> p (a b)"), ps[:, 1, :], ACT.Copy).then_inc(s.hT_copied, 1)
                f(acc[:, c, :], h[:, c, :], ACT.Copy, scale=ALPHA).then_inc(s.acc_init, 1)

            for c in range(TT + 3):
                if 3 <= c:
                    h_transposed(c - 3)
                if c < TT:
                    mix_transposed(c)
                if 2 <= c < TT + 2:
                    deviation(c - 2)
            act.wait_ge(s.h_ready, TT)
            for i, name in enumerate(("ln2_g", "ln2_b")):
                act.dma_start(lnrow[:, i, :], A[name][0].partition_broadcast(P)).then_inc(s.ln_loaded, 16)
            act.wait_ge(s.max_ready, 1)
            for c in range(TT):
                r = f(ex_t[:, c, :], logit[:, c, :], ACT.Exp, bias=sm[:, 1, c:c + 1], accum_out=sm[:, 2, c:c + 1])
            r.then_inc(s.rexp_done, 1)
            act.wait_ge(s.affT_ps, 1)
            f(affT, ps[0:EXPERTS, 3, :], ACT.Copy).then_inc(s.affT_copied, 1)
            act.wait_ge(s.slot_ps, 1)
            f(slotv, ps[:, 4, 0:TT * EXPERTS].rearrange("p (c e) -> p c e", c=TT), ACT.Copy).then_inc(s.slots_ready, 1)
            with act.Fori(0, EXPERTS // 4) as it:
                for u in range(2):
                    for j in range(2):
                        act.wait_ge(s.xin_ps, 4 * it + 2 * u + j + 1)
                        f(xin[:, 4 * j:4 * j + 4, :].rearrange("p a b -> p (a b)"), ps[:, 5 + j, :], ACT.Copy).then_inc(s.xin_copied, 1)
                    act.wait_ge(s.selT_ps, 2 * it + u + 1)
                    f(selgT.rearrange("p a b -> p (a b)"), ps[:, 7, :], ACT.Copy).then_inc(s.selT_copied, 1)
                    for c in range(NCH):
                        i = NCH * u + c
                        act.wait_ge(w_used[3], 2 * NCH * it + i + 3)
                        f(s_h1[:, i % 2, :], ps[:, i % 2, 0:256], ACT.Silu).then_inc(s.silu_pair, 1)
                        act.wait_ge(s.hidT_ps, 2 * NCH * it + i + 1)
                        f(hidT[:, i % 2].rearrange("p a b -> p (a b)"), ps[:, 2, 256 * (i % 2):256 * (i % 2) + 256], ACT.Copy).then_inc(s.hidT_copied, 1)
                    act.wait_ge(w_used[5], 2 * NCH * it + NCH * (u + 1) + 2)
                    for j in range(2):
                        f(ye[:, 512 * j:512 * j + 512], ps[:, 3 + j, :], ACT.Copy).then_inc(s.ye_copied, 1)
            act.wait_ge(s.ln2_var, TT)
            f(mv[:, :, 2:3], mv[:, :, 1:2], ACT.Sqrt, bias=eps_col).then_inc(s.ln2_std, 1)

        @block.tensor
        def _(pe):
            def mm(out, lhsT, rhs, a, z):
                return pe.matmul(out, lhsT, rhs, start=a, stop=z)

            used = [0]

            def slice_wait():
                i = used[0]
                pe.wait_ge(slice_loaded[i % NW], 16 * (i // NW + 1))
                used[0] += 1
                return wring[:, i % NW]

            def before(m, c):
                sigmoids, products = (0, 3), (1, 2, 4, 5)
                if m in sigmoids:
                    return s.mix_sig, sigmoids.index(m) * TT + c + 1
                return s.mix_read, products.index(m) * TT + c + 1

            pe.wait_ge(s.consts_ready, 8)
            for i in range(2 * TT):
                c, j = divmod(i, 2)
                pe.wait_ge(x_loaded[c], 16)
                if i >= 2:
                    pe.wait_ge(s.xT_copied, i - 1)
                for k in range(4):
                    r = pe.transpose(ps[:, i % 2, P * k:P * k + P], x_nat[:, c, P * (4 * j + k):P * (4 * j + k + 1)], ident)
                r.then_inc(s.xT_ps, 1)
            def parameters_transposed():
                pe.wait_ge(s.params_loaded, 16 * PARAMS)
                pe.wait_ge(s.ls_filled, 1)
                for r in range(2):
                    for q in range(GP // 8):
                        pe.transpose(ps[:, 2 + r, P * q:P * q + P], c_nat[:, q, r, :], ident)
                for i in range(6):
                    pe.transpose(ps[:, 4, GP * i:GP * i + GP], par_raw[:, i, :], ident[0:GP, 0:GP])
                pe.transpose(ps[:, 4, 144:264], vec_a, ident[0:120, 0:120])
                pe.transpose(ps[:, 4, 264:276], vec_b, ident[0:12, 0:12])
                pe.transpose(ps[0:2 * S5_K, 4, 276:300], vec_d, ident[0:GP, 0:GP]).then_inc(s.vec_ps, 1)

            pe.wait_ge(s.xT_copied, KT)
            for i in range(S5_W // P):
                if i in U_SLICES:
                    w, i0 = slice_wait(), i
                if i == 1:
                    parameters_transposed()
                if i >= 2:
                    pe.wait_ge(s.u_copied, i - 1)
                for k in range(KT):
                    r = mm(ps[:, i % 2, :], w[:, k, P * (i - i0):P * (i - i0) + P], xT[:, k, :], k == 0, k == KT - 1)
                r.then_inc(s.u_ps, 1)
            w = slice_wait()
            for c in range(TT):
                for k in range(KT):
                    r = mm(ps[:, 5, 48 * c:48 * c + 48], xT[:, k, P * c:P * c + P], w[:, k, 0:48], k == 0, k == KT - 1)
            r.then_inc(s.dt_ps, 1)
            gate_w = [None]

            def gate(t, bank):
                if t % TT == 0:
                    gate_w[0] = slice_wait()
                c = t % TT
                for k in range(KT):
                    r = mm(ps[:, bank, :], xT[:, k, P * c:P * c + P], gate_w[0][:, k, :], k == 0, k == KT - 1)
                r.then_inc(s.gate_ps, 1)

            pe.wait_ge(s.u_copied, 6)
            for t in range(2):
                gate(t, t % 2)
            pe.wait_ge(s.da_ready, 1)
            H = HEADS
            for i, (m, c0) in enumerate(((m_le, 0), (m_ge, H), (m_gt, 0), (m_lt, H))):
                mm(ps[:, 5, 96 * i:96 * i + 96].rearrange("p (c h) -> p c h", c=TT), m, da[:, :, c0:c0 + H], True, True)
            mm(ps[:, 6, 0:8 * H].rearrange("p (c h) -> p c h", c=TT), ones, da, True, True).then_inc(s.seg_ps, 1)

            def toeplitz(q):
                pe.wait_ge(s.bd_ready, q + 1)
                if q >= 1:
                    pe.wait_ge(s.toep_built, q)
                    pe.wait_ge(s.gate_copied, gates_before[q] - 1)
                for d in range(2):
                    i0 = 0 if d == 0 else S5_K
                    for g in range(QB):
                        at = (d * QB + g) * 64
                        for r in range(2):
                            ins = mm(ps[0:32, 4, at:at + 64], bpad[:, g, d, r, :], vc[:, q % 2, g, d, r, i0:i0 + 64], r == 0, r == 1)
                ins.then_inc(s.toep_ps, 1)

            def states(q):
                pe.wait_ge(s.bd_ready, q + 1)
                pe.wait_ge(s.u_loaded, 16 * 2 * T)
                if q >= 1:
                    pe.wait_ge(s.F_read, 2 * q)
                for g in range(QB + 1):
                    if g < QB:
                        i = QB * q + g
                        if i >= 2:
                            pe.wait_ge(s.wT_copied, i - 1)
                        for k in range(4):
                            r = pe.transpose(ps[:, 5 + i % 2, P * k:P * k + P], wbd[:, g, k // 2, k % 2, :], ident)
                        r.then_inc(s.wT_ps, 1)
                    if g >= 1:
                        i = QB * q + g - 1
                        pe.wait_ge(s.wT_copied, i + 1)
                        for k in range(4):
                            r = mm(ps[:, k, P * (g - 1):P * g], wT[:, i % 2, k, :], U[:, i, :], True, True)
                        r.then_inc(s.F_ps, 1)

            def outputs(q):
                pe.wait_ge(s.X_ready, 2 * (q + 1))
                pe.wait_ge(s.toep_loaded, 16 * 2 * T * (q + 1))
                if gates_before[q] < GATES:
                    pe.wait_ge(s.gate_copied, gates_before[q + 1])
                if q >= 1:
                    pe.wait_ge(s.y5_copied, q)
                for g in range(QB):
                    o = ps[:, 7, P * g:P * g + P]
                    mm(o, M[:, QB * q + g, :], U[:, QB * q + g, :], True, False)
                    for k in range(4):
                        r = mm(o, vbd[:, q % 2, g, k // 2, k % 2, :], X[:, q % 2, k // 2, k % 2, g, :], False, k == 3)
                r.then_inc(s.y5_ps, 1)

            pe.wait_ge(s.seg_exp, 1)
            pe.wait_ge(s.gate_copied, EARLY)
            for q in range(NQ):
                toeplitz(q)
                states(q)
                if q >= 1:
                    outputs(q - 1)
                for t in range(gates_before[q], gates_before[q + 1]):
                    if t >= gates_before[q] + 2:
                        pe.wait_ge(s.gate_copied, t - 1)
                    elif t % 2 == 0:
                        pe.wait_ge(s.toep_built, q + 1)
                    elif q >= 1:
                        pe.wait_ge(s.y5_copied, q)
                    gate(t, (4, 7)[t % 2])
            pe.wait_ge(s.F_read, 2 * NQ)
            for b in range(XBC // 512 + 1):
                if b < XBC // 512:
                    w = slice_wait()
                    for j in range(4):
                        i = 4 * b + j
                        if i == 2:
                            outputs(NQ - 1)
                        if i >= 2:
                            pe.wait_ge(s.xbc_raw, i - 1)
                        for k in range(KT):
                            r = mm(ps[:, i % 2, :], w[:, k, P * j:P * j + P], xT[:, k, :], k == 0, k == KT - 1)
                        r.then_inc(s.xbc_ps, 1)
                for j in range(4):
                    i = 4 * (b - 1) + j
                    if 0 <= i < 16:
                        pe.wait_ge(s.silu_done, i + 1)
                        if i >= 2:
                            pe.wait_ge(s.nat_copied, i - 1)
                        src = xc[:, j, :] if i < 12 else bT[:, i - 12, :]
                        for c in range(TT):
                            r = pe.transpose(ps[:, 2 + i % 2, P * c:P * c + P], src[:, P * c:P * c + P], ident)
                        r.then_inc(s.nat_ps, 1)

            def z_tile(g, c, w):
                t = g * TT + c
                if t >= 2:
                    pe.wait_ge(s.z_silu, t)
                for k in range(KT):
                    r = mm(ps[:, int(t == 1), 0:GI], xT[:, k, P * c:P * c + P], w[:, k, 0:GI], k == 0, k == KT - 1)
                r.then_inc(s.z_ps, 1)

            def added_states(g, j):
                for d, c in ((0, j), (1, TT - 1 - j)):
                    i = 6 * g + 2 * j + d
                    pe.wait_ge(s.xw_ready, i + 1)
                    if i >= 2:
                        pe.wait_ge(s.carried, i - 1)
                    mm(ps[:, 6 + d, 0:GI], bn[:, c, P * g:P * g + P], xw[:, d, :], True, True).then_inc(s.st_ps, 1)

            def scores_and_segments(i):
                g, c = divmod(i, TT)
                q = slice(P * c, P * c + P)
                if i >= 1:
                    pe.wait_ge(s.g_ready, i)
                mm(ps[:, 4, 0:P], bT[:, g, q], cT[:, g, q], True, True).then_inc(s.cb_ps, 1)
                pe.wait_ge(s.mats_ready, 2 * i + 1)
                if i >= 1:
                    pe.wait_ge(s.segm_exp, i)
                for a in range(2):
                    o = ps[:, 2 + a, 0:GI].rearrange("p (h q) -> p h q", h=3)
                    mm(o, m_gt, rhs_f[:, 3 * a:3 * a + 3, :], True, False)
                    r = mm(o, m_lt, rhs_b[:, 3 * a:3 * a + 3, :], False, True)
                r.then_inc(s.segm_ps, 1)

            def y_products(i):
                g, c = divmod(i, TT)
                q = slice(P * c, P * c + P)
                ahead = 2 * min(c, TT - 1) if g + 1 < GROUPS else 0
                pe.wait_ge(s.carried, 6 * (g + 1) + ahead)
                if i >= 1:
                    pe.wait_ge(s.y_read, i)
                if c >= 1:
                    mm(ps[:, 6, 0:GI], cT[:, g, q], st[:, g % 2, 0, c - 1, :], True, True)
                if c < TT - 1:
                    mm(ps[:, 7, 0:GI], cT[:, g, q], st[:, g % 2, 1, c, :], True, True)
                pe.wait_ge(s.g_ready, i + 1)
                for j in range(HG):
                    h0 = GI * g + HEADDIM * j
                    r = mm(ps[:, 5, HEADDIM * j:HEADDIM * j + HEADDIM], gmat[:, i % 2, j, :], xs[:, c, h0:h0 + HEADDIM], True, True)
                r.then_inc(s.yd_ps, 1)

            def y_transposed(i):
                pe.wait_ge(s.yn_ready, i + 1)
                if i >= 1:
                    pe.wait_ge(s.yt_copied, 3 * i)
                for j in range(3):
                    r = pe.transpose(ps[:, 1, P * j:P * (j + 1)], ty[:, 4, P * j:P * j + P], ident)
                r.then_inc(s.yt_ps, 1)

            w = slice_wait()
            pe.wait_ge(s.xbc_raw, 20)
            z_tile(0, 0, w)
            pe.wait_ge(s.silu_done, 17)
            pe.wait_ge(s.nat_copied, 16)
            scores_and_segments(0)
            pe.wait_ge(s.silu_done, 20)
            for j in range(TT - 1):
                added_states(0, j)
                if j + 1 < Z_AHEAD:
                    z_tile(0, j + 1, w)
            pe.wait_ge(s.z_silu, 2)
            for i in range(GROUPS * TT):
                g, c = divmod(i, TT)
                if i + 1 < GROUPS * TT:
                    scores_and_segments(i + 1)
                y_products(i)
                if i >= 1:
                    y_transposed(i - 1)
                if i + Z_AHEAD < GROUPS * TT:
                    if (i + Z_AHEAD) % TT == 0:
                        w = slice_wait()
                    z_tile(*divmod(i + Z_AHEAD, TT), w)
                if g + 1 < GROUPS and c < TT - 1:
                    pe.wait_ge(s.y_read, i + 1)
                    added_states(g + 1, c)
            nk = 6
            for m in range(6):
                lhs, halves = (yT, 2) if m % 3 == 2 else (ysT, 1)
                if m == 0:
                    pe.wait_ge(s.ysT_ready, S5_W // P)
                    pe.wait_ge(s.z_silu, GROUPS * TT)
                    pe.wait_ge(s.segm_exp, GROUPS * TT)
                    pe.wait_ge(s.g_ready, GROUPS * TT)
                if m == 1:
                    y_transposed(GROUPS * TT - 1)
                    pe.wait_ge(s.yt_copied, 3 * GROUPS * TT)
                    pe.wait_ge(s.y_read, GROUPS * TT)
                for half in range(halves):
                    w = slice_wait()
                    for c in range(TT):
                        if half == 0 and m >= 2:
                            pe.wait_ge(*before(m - 2, c))
                        for kk in range(nk):
                            r = mm(ps[:, m_bank[m % 2][c], :], lhs[:, nk * half + kk, P * c:P * c + P], w[:, kk, :],
                                   half == 0 and kk == 0, half == halves - 1 and kk == nk - 1)
                        if half == halves - 1:
                            r.then_inc(s.mix_ps, 1)
                        elif c == TT - 1:
                            r.then_inc(s.slice_used, 1)
            w_o = []

            def mix_transposed(c):
                pe.wait_ge(s.mix_ready, TT + c + 1)
                if c == 0:
                    pe.wait_ge(*before(4, TT - 1))
                else:
                    pe.wait_ge(s.mixT_copied, 2 * c)
                for j in range(2):
                    for k in range(4):
                        kk = 4 * j + k
                        r = pe.transpose(ps[:, 2 * j, P * k:P * k + P], mix[:, c, P * kk:P * kk + P], ident)
                    r.then_inc(s.mixT_ps, 1)

            def out_product(c):
                pe.wait_ge(s.mixT_copied, 2 * (c + 1))
                if c == 1:
                    pe.wait_ge(s.mix_read, 4 * TT)
                if c >= 2:
                    pe.wait_ge(s.wo_read, 2 * (c - 1))
                for j in range(2):
                    if c == 0:
                        w_o.append(slice_wait())
                    for k in range(KT):
                        r = mm(ps[:, o_bank[c % 2][j], :], mixT[:, c % 2, k, :], w_o[j][:, k, :], k == 0, k == KT - 1)
                    r.then_inc(s.wo_ps, 1)

            def router(c):
                pe.wait_ge(s.h_ready, c + 1)
                for j in range(2):
                    if 2 * c + j >= 1:
                        pe.wait_ge(s.hT_copied, 2 * c + j)
                    for k in range(4):
                        kk = 4 * j + k
                        r = pe.transpose(ps[:, 1, P * k:P * k + P], h[:, c, P * kk:P * kk + P], ident)
                    r.then_inc(s.hT_ps, 1)
                pe.wait_ge(s.hT_copied, 2 * (c + 1))
                pe.wait_ge(s.wr_loaded, 16)
                for k in range(KT):
                    r = mm(ps[:, 5, EXPERTS * c:EXPERTS * c + EXPERTS], hT[:, k, :], w_r[:, k, :], k == 0, k == KT - 1)
                r.then_inc(s.logit_ps, 1)

            for c in range(TT + 3):
                if 3 <= c:
                    router(c - 3)
                if c < TT:
                    mix_transposed(c)
                if 1 <= c <= TT:
                    out_product(c - 1)
                if c == 1:
                    pe.wait_ge(s.mix_ready, 2 * TT)
                    for k in range(6):
                        pe.nop().then_inc(w_used[k], 2)
            pe.wait_ge(s.aff_ready, 1)
            for c in range(TT):
                r = pe.transpose(ps[0:EXPERTS, 3, P * c:P * c + P], aff[:, c, :], ident)
            r.then_inc(s.affT_ps, 1)
            pe.wait_ge(s.slotT_ready, 1)
            for c in range(TT):
                r = pe.transpose(ps[:, 4, EXPERTS * c:EXPERTS * c + EXPERTS], cum[:, P * c:P * c + P], ident[0:EXPERTS, 0:EXPERTS])
            r.then_inc(s.slot_ps, 1)
            with pe.Fori(0, EXPERTS // 4) as it:
                for u in range(2):
                    pair = 2 * it + u
                    pe.wait_ge(s.sel_built, pair + 1)
                    for j in range(2):
                        for k in range(4):
                            for c in range(TT):
                                kk = 4 * j + k
                                r = mm(ps[:, 5 + j, P * k:P * k + P], h[:, c, P * kk:P * kk + P],
                                       sel[:, c].rearrange("p a b -> p (a b)"), c == 0, c == TT - 1)
                        r.then_inc(s.xin_ps, 1)

                    def hidden(i, which):
                        for e in range(2):
                            pe.wait_ge(w_loaded[2 * which + e][i % 2], 16 * NCH * it + 16 * (i // 2 + 1))
                        for k in range(KT):
                            if i == NCH * u and which == 0 and k % 4 == 0:
                                pe.wait_ge(s.xin_copied, 2 * pair + 1 + k // 4)
                            for e in range(2):
                                w = ring[:, 2 * which + e, i % 2].rearrange("p (k f) -> p k f", k=KT)
                                r = mm(ps[64 * e:64 * e + 64, i % 2, FC * which:FC * which + FC],
                                       xin[:, k, 64 * e:64 * e + 64], w[:, k, :], k == 0, k == KT - 1)
                                if k == KT - 1:
                                    r.then_inc(w_used[2 * which + e], 1)
                        return r

                    def turn(i):
                        pe.wait_ge(s.hid_ready, 2 * NCH * it + i + 1)
                        for j in range(2):
                            r = pe.transpose(ps[:, 2, 256 * (i % 2) + P * j:256 * (i % 2) + P * j + P], hid[:, i % 2, P * j:P * j + P], ident)
                        r.then_inc(s.hidT_ps, 1)

                    def down(i, c):
                        pe.wait_ge(s.hidT_copied, 2 * NCH * it + i + 1)
                        for e in range(2):
                            pe.wait_ge(w_loaded[4 + e][i % 2], 16 * NCH * it + 16 * (i // 2 + 1))
                        for j in range(2):
                            for n in range(2):
                                for e in range(2):
                                    w = ring[:, 4 + e, i % 2].rearrange("p (j d) -> p j d", j=2)
                                    r = mm(ps[64 * e:64 * e + 64, 3 + n, :], hidT[:, i % 2, j, 64 * e:64 * e + 64],
                                           w[:, j, 512 * n:512 * n + 512], c == 0 and j == 0, c == NCH - 1 and j == 1)
                                    if j == 1 and n == 1:
                                        r.then_inc(w_used[4 + e], 1)

                    for c in range(NCH):
                        i = NCH * u + c
                        if i >= 2:
                            pe.wait_ge(s.hid_ready, 2 * NCH * it + i - 1)
                        hidden(i, 0)
                        if c >= 1:
                            turn(i - 1)
                        else:
                            pe.wait_ge(s.sel_ready, pair + 1)
                            for k in range(TT):
                                r = pe.transpose(ps[:, 7, P * k:P * k + P], selg[:, k].rearrange("p a b -> p (a b)"), ident)
                            r.then_inc(s.selT_ps, 1)
                        hidden(i, 1)
                        if c >= 1:
                            down(i - 1, c - 1)
                    turn(NCH * u + NCH - 1)
                    down(NCH * u + NCH - 1, NCH - 1)
                    pe.wait_ge(s.selT_copied, pair + 1)
                    for k in range(2 * TT):
                        c, j = divmod(k, 2)
                        if k < 2:
                            pe.wait_ge(s.ye_copied, 2 * pair + k + 1)
                        else:
                            pe.wait_ge(s.acc_added, 2 * TT * pair + k - 1)
                        mm(ps[:, 5 + k % 2, :], selgT[:, c, :], ye[:, 512 * j:512 * j + 512], True, True).then_inc(s.sc_ps, 1)
                    pe.wait_ge(s.acc_added, 2 * TT * pair + 2 * TT)

        @block.vector
        def _(dve):
            n = Steps(dve, s.dve_step)
            tt, ts, stt = dve.tensor_tensor, dve.tensor_scalar, dve.scalar_tensor_tensor

            def reduce_phase(out, x, k, tmp, ready=None):
                n.link(ts(k, x, 1.0 / TWO_PI, ROUND, ALU.mult, ALU.add))
                n.link(ts(k, k, -ROUND, None, ALU.add))
                n.link(stt(tmp, k, -PI_1, x, ALU.mult, ALU.add))
                n.link(stt(out, k, -PI_2, tmp, ALU.mult, ALU.add))
                n.link(stt(tmp, k, -PI_3, out, ALU.mult, ALU.add))
                r = ts(out, tmp, PI_LIM, -PI_LIM, ALU.min, ALU.max)
                if ready is None:
                    n.link(r)
                else:
                    r.then_inc(ready, 1)
                    dve.wait_ge(ready, 1)

            def cmul(o_re, o_im, a_re, a_im, b_re, b_im, t):
                tt(t[0], a_re, b_re, ALU.mult)
                tt(t[1], a_im, b_im, ALU.mult)
                tt(t[2], a_re, b_im, ALU.mult)
                n.link(tt(t[3], a_im, b_re, ALU.mult))
                tt(o_re, t[0], t[1], ALU.subtract)
                n.link(tt(o_im, t[2], t[3], ALU.add))

            def maps(q):
                gs = slice(QB * q, QB * q + QB)
                if q >= 1:
                    dve.wait_ge(s.v_ready, q)
                if q >= 2:
                    dve.wait_ge(s.toep_ps, q - 1)
                    dve.wait_ge(s.bd_ready, q - 1)
                tv = [x.rearrange("p g c -> p (g c)")[:, 0:QB * 80].rearrange("p (g i k) -> p g i k", g=QB, k=S5_K) for x in (zr, zi, t1, t2)]
                for d in range(2):
                    powers = pt[:, d, :, d, gs, :]
                    out = vc[:, q % 2]
                    c_re, c_im = (mid2(c_map[:, r, gs, :], T + 1) for r in range(2))
                    p_re, p_im = (last(powers[:, r], S5_K) for r in range(2))
                    for t, (x, y) in enumerate(((p_re, c_re), (p_im, c_im), (p_re, c_im), (p_im, c_re))):
                        n.done(tt(tv[t], x, y, ALU.mult))
                    n.wait()
                    n.done(tt(out[:, :, d, 0, :].rearrange("p g (i k) -> p g i k", k=S5_K), tv[0], tv[1], ALU.subtract))
                    ins = stt(out[:, :, d, 1, :], tv[2].rearrange("p g i k -> p g (i k)"), -1.0,
                               tv[3].rearrange("p g i k -> p g (i k)"), ALU.mult, ALU.subtract)
                    if d == 0:
                        n.link(ins)
                    else:
                        ins.then_inc(s.v_ready, 1)
                        n.wait()
                        dve.wait_ge(s.v_ready, q + 1)

            for i in range(2 * TT):
                c, j = divmod(i, 2)
                dve.wait_ge(s.xT_ps, i + 1)
                dve.tensor_copy(xT[:, 4 * j:4 * j + 4, P * c:P * c + P],
                                ps[:, i % 2, :].rearrange("p (a b) -> p a b", a=4)).then_inc(s.xT_copied, 1)
            dve.wait_ge(s.params_loaded, 16 * PARAMS)
            for d in range(2):
                r = dve.tensor_copy(par_raw[:, 3 * d + 2, :].rearrange("g (b p) -> g b p", b=2), last(ls_raw[:, d, :], S5_P))
            r.then_inc(s.ls_filled, 1)
            dve.wait_ge(s.vec_ps, 1)
            for r in range(2):
                n.done(dve.tensor_copy(c_map[:, r].rearrange("p g k -> p (g k)"), ps[:, 2 + r, 0:GP * S5_K]))
            n.done(dve.tensor_copy(conv_w, ps[:, 4, 144:244].rearrange("p (k t) -> p t k", k=CONV)))
            n.done(dve.tensor_copy(conv_b, ps[:, 4, 244:264]))
            n.done(dve.tensor_copy(norm_g, ps[:, 4, 264:276]))
            n.done(dve.tensor_copy(d_col, ps[0:32, 4, 276:300]))
            n.done(tt(eye2, ident[0:32, 0:16], ident[0:32, 16:32], ALU.add))
            dve.tensor_copy(par.rearrange("p a b c -> p (a b c)"), ps[:, 4, 0:6 * GP]).then_inc(s.par_ready, 1)
            dve.wait_ge(s.par_ready, 1)
            n.wait()
            n.done(tt(d_diag, first(eye2, GP), last(d_col, S5_K), ALU.mult))
            a_re, a_im = par[:, :, 0, :], par[:, :, 1, :]
            v = lambda i: small[:, i]
            dve.wait_ge(s.step_exp, 1)
            tt(v(1), a_re, v(0), ALU.mult).then_inc(s.lr_ready, 1)
            n.link(tt(v(2), a_im, v(0), ALU.mult))
            reduce_phase(v(4), v(2), v(7), v(8), s.theta_ready)
            dve.wait_ge(s.tanh_done, 1)
            n.link(ts(v(10), v(3), -1.0, 1.0, ALU.mult, ALU.add))
            n.link(dve.reciprocal(v(11), v(10)))
            n.link(stt(v(12), v(3), 2.0, v(11), ALU.mult, ALU.mult))
            n.link(ts(v(13), v(12), 1.0, None, ALU.add))
            dve.wait_ge(s.sin_done, 1)
            n.link(stt(v(14), v(6), 2.0, v(6), ALU.mult, ALU.mult))
            n.link(ts(v(15), v(14), -1.0, 1.0, ALU.mult, ALU.add))
            n.link(tt(v(16), v(12), v(15), ALU.mult))
            n.done(tt(v(17), v(16), v(14), ALU.subtract))
            n.done(tt(v(18), v(13), v(5), ALU.mult))
            n.done(tt(v(19), v(13), v(15), ALU.mult))
            tt(v(20), a_re, a_re, ALU.mult)
            n.link(tt(v(21), a_im, a_im, ALU.mult))
            n.link(tt(v(22), v(20), v(21), ALU.add))
            n.done(dve.reciprocal(v(23), v(22)))
            n.done(ts(v(24), a_im, -1.0, None, ALU.mult))
            n.wait()
            cmul(v(25), v(26), v(17), v(18), a_re, v(24), [small[:, 27 + i] for i in range(4)])
            n.done(tt(v(25), v(25), v(23), ALU.mult))
            n.done(tt(v(26), v(26), v(23), ALU.mult))
            n.wait()
            dve.wait_ge(s.b_loaded, 32)
            tb = [vc.rearrange("p a b c d e -> p (a b c d e)")[:, GP * S5_K * i:GP * S5_K * (i + 1)].rearrange("p (g k) -> p g k", g=GP)
                  for i in range(4)]
            for d in range(2):
                q_re, q_im = last(small[:, 25, d], S5_K), last(small[:, 26, d], S5_K)
                cmul(bbar[:, d, 0], bbar[:, d, 1], q_re, q_im, b_raw[:, 0], b_raw[:, 1], tb)
            n.done(dve.memset(X[:, 0, 0, :, :, 0:1], 0.0))
            n.done(dve.memset(X[:, 1, 0, :, :, 0:1], 0.0))
            n.done(dve.memset(X[:, 0, 1, :, :, NC - 1:NC], 0.0))
            n.done(dve.memset(X[:, 1, 1, :, :, NC - 1:NC], 0.0))
            pw = [[pt[:, 0, r, :, :, j] for r in range(2)] for j in range(T + 1)]
            n.done(dve.memset(pw[0][0], 1.0))
            n.done(dve.memset(pw[0][1], 0.0))
            n.done(dve.tensor_copy(pw[1][0], v(19)))
            n.done(dve.tensor_copy(pw[1][1], v(18)))
            n.wait()
            tp = [small[:, 27 + i] for i in range(4)]
            cmul(*pw[2], *pw[1], *pw[1], tp)
            cmul(*pw[3], *pw[2], *pw[1], tp)
            cmul(*pw[4], *pw[2], *pw[2], tp)
            for j in range(T + 1):
                for r in range(2):
                    n.done(dve.tensor_copy(pt[:, 1, r, :, :, T - j], pw[j][r]))
            n.link(tt(v(7), v(13), v(13), ALU.mult))
            n.link(tt(v(20), v(7), v(7), ALU.mult))
            n.link(ts(v(21), v(4), float(T), None, ALU.mult))
            reduce_phase(v(22), v(21), v(7), v(8))
            modulus, phase = v(20), v(22)
            for k in range(LEVELS):
                n.done(ts(zr.rearrange("p g c -> p (g c)")[:, 2 * GP * k:2 * GP * (k + 1)],
                          phase.rearrange("p d g -> p (d g)"), float(2 ** k), None, ALU.mult))
            n.wait()
            flat_part = lambda x: x.rearrange("p g c -> p (g c)")[:, 0:LEVELS * 2 * GP]
            reduce_phase(ang, flat_part(zr), flat_part(sr), flat_part(si), s.rot_angle)

            maps(0)
            dve.wait_ge(s.rot_sin, 1)
            n.link(stt(rot_flat[0], ang_half, -2.0, ang_half, ALU.mult, ALU.mult))
            ts(rot_flat[0], rot_flat[0], 1.0, None, ALU.add).then_inc(s.rot_ready, 1)
            state_maps(dve, n, [x.rearrange("p g c -> p (g c)")[:, 0:QB * 64] for x in (zr, zi, t1, t2)], 0)

            dve.wait_ge(s.dt_ps, 1)
            dve.wait_ge(s.broadcasts_loaded, 80)
            n.link(tt(dtime, ps[:, 5, 0:TT * 2 * HEADS].rearrange("p (c h) -> p c h", c=TT), first(dt_bias, TT), ALU.add))
            stt(w_end, dtime, -1.0, dtime, ALU.mult, ALU.max).then_inc(s.dt_abs, 1)
            dve.wait_ge(s.dt_ln, 2)
            n.link(stt(dtime, dtime, 0.0, w_end, ALU.max, ALU.add))
            dve.scalar_tensor_tensor(da, dtime, -1.0, first(a_neg, TT), ALU.mult, ALU.mult).then_inc(s.da_ready, 1)

            def toeplitz_rows(q):
                dve.wait_ge(s.toep_ps, q + 1)
                if q >= 1:
                    dve.wait_ge(s.toep_stored, 16 * q)
                k = ps[0:32, 4, :].rearrange("p (d g i k) -> p d g i k", d=2, g=QB, k=S5_K)
                o = toep
                dve.tensor_copy(o[:, :, 0:T - 1, :], k[:, 1, :, 0:T - 1, :])
                dve.tensor_copy(o[:, :, T:, :], k[:, 0, :, 1:, :])
                n.link(tt(o[:, :, T - 1, :], k[:, 1, :, T - 1, :], d_diag[:, QB * q:QB * q + QB, :], ALU.add))
                tt(o[:, :, T - 1, :], o[:, :, T - 1, :], k[:, 0, :, 0, :], ALU.add).then_inc(s.toep_built, 1)

            def recur(q, d):
                dve.wait_ge(s.F_ps, QB * (q + 1))
                dve.wait_ge(s.tab_ready, 2 * q + d + 1)
                if q >= 2:
                    dve.wait_ge(s.y5_ps, q - 1)
                F = [ps[:, 2 * d + r, :].rearrange("p (g c) -> p g c", g=QB) for r in range(2)]
                if d == 1:
                    F = [x[:, :, ::-1] for x in F]
                c, sn = cos_t[:, d], sin_t[:, d]
                flat = lambda x: x.rearrange("p g c -> p (g c)")
                tt(zr, F[0], c, ALU.mult)
                tt(zi, F[1], c, ALU.mult)
                tt(t1, F[1], sn, ALU.mult)
                n.link(tt(t2, F[0], sn, ALU.mult))
                tt(zr, zr, t1, ALU.add)
                tt(zi, zi, t2, ALU.subtract).then_inc(s.F_read, 1)
                dve.wait_ge(s.F_read, 2 * q + d + 1)
                for g in range(QB):
                    decay = modulus[:, d, QB * q + g:QB * q + g + 1].to_broadcast([P, NC])
                    n.done(dve.tensor_tensor_scan(sr[:, g], decay, zr[:, g], 0.0, ALU.mult, ALU.add))
                    n.done(dve.tensor_tensor_scan(si[:, g], decay, zi[:, g], 0.0, ALU.mult, ALU.add))
                n.wait()
                tt(zr, sr, c, ALU.mult)
                tt(zi, sr, sn, ALU.mult)
                tt(t1, si, sn, ALU.mult)
                n.link(tt(t2, si, c, ALU.mult))
                L = NC - 1
                for r, (x, y, op) in enumerate(((zr, t1, ALU.subtract), (zi, t2, ALU.add))):
                    o = X[:, q % 2, d, r]
                    o = o[:, :, 1:] if d == 0 else o[:, :, 0:L][:, :, ::-1]
                    ins = tt(o, x[:, :, 0:L], y[:, :, 0:L], op)
                ins.then_inc(s.X_ready, 1)
                dve.wait_ge(s.X_ready, 2 * q + d + 1)

            for q in range(NQ):
                if q + 1 < NQ:
                    maps(q + 1)
                if q == 0:
                    dve.wait_ge(s.seg_exp, 1)
                    n.done(tt(w_end, w_end, dtime, ALU.mult))
                toeplitz_rows(q)
                if q + 1 < NQ:
                    state_maps(dve, n, [x.rearrange("p g c -> p (g c)")[:, 0:QB * 64] for x in (zr, zi, t1, t2)], q + 1)
                for d in range(2):
                    recur(q, d)
            dve.wait_ge(s.y5_ps, NQ)
            half = CONV // 2
            n.done(dve.memset(xraw[:, :, 0:half], 0.0))
            n.done(dve.memset(xraw[:, :, half + SEQ:], 0.0))
            for b in range(XBC // 512):
                n.wait()
                for j in range(4):
                    i = 4 * b + j
                    for k in range(CONV):
                        if k == 0:
                            dve.wait_ge(s.xbc_raw, i + 1)
                            if b >= 1:
                                dve.wait_ge(s.silu_done, i - 3)
                            r = ts(cacc[:, j], xraw[:, j, 0:SEQ], conv_w[:, i, 0:1], conv_b[:, i:i + 1], ALU.mult, ALU.add)
                        else:
                            dve.wait_ge(s.conv_tap, (CONV - 1) * i + k)
                            r = stt(cacc[:, j], xraw[:, j, k:k + SEQ], conv_w[:, i, k:k + 1], cacc[:, j], ALU.mult, ALU.add)
                        r.then_inc(s.conv_tap if k < CONV - 1 else s.conv_done, 1)
            n.wait()
            dve.wait_ge(s.nat_copied, 16)
            dve.wait_ge(s.silu_done, 20)
            bc = lambda x: last(x, HEADDIM)
            h3 = lambda x: x.rearrange("p (h w) -> p h w", h=HG)

            def weighted_x(g, j):
                for d, c in ((0, j), (1, TT - 1 - j)):
                    i = 6 * g + 2 * j + d
                    if i >= 2:
                        dve.wait_ge(s.st_ps, i - 1)
                    h0 = d * HEADS + HG * g
                    tt(h3(xw[:, d]), h3(xs[:, c, GI * g:GI * g + GI]), bc(w_end[:, c, h0:h0 + HG]), ALU.mult).then_inc(s.xw_ready, 1)

            def carry(g, j):
                for d, c in ((0, j), (1, TT - 1 - j)):
                    i = 6 * g + 2 * j + d
                    h0 = d * HEADS + HG * g
                    to = st[:, g % 2, d, j if d == 0 else TT - 2 - j]
                    if j:
                        was = st[:, g % 2, d, j - 1 if d == 0 else TT - 1 - j]
                        dve.wait_ge(s.carried, i - 1)
                        n.link(tt(h3(to), h3(was), bc(e_all[:, c, h0:h0 + HG]), ALU.mult))
                        dve.wait_ge(s.st_ps, i + 1)
                        tt(to, to, ps[:, 6 + d, 0:GI], ALU.add).then_inc(s.carried, 1)
                    else:
                        dve.wait_ge(s.st_ps, i + 1)
                        dve.tensor_copy(to, ps[:, 6 + d, 0:GI]).then_inc(s.carried, 1)

            def mixing_matrix(i):
                dve.wait_ge(s.segm_exp, i + 1)
                dve.wait_ge(s.cb_ps, i + 1)
                if i >= 2:
                    dve.wait_ge(s.yd_ps, i - 1)
                o = gmat[:, i % 2]
                n.link(tt(o, emat, first(ps[:, 4, 0:P], HG), ALU.mult))
                dve.wait_ge(s.mats_ready, 2 * i + 2)
                tt(o, o, dmat, ALU.mult).then_inc(s.g_ready, 1)

            for j in range(TT - 1):
                weighted_x(0, j)
                if j == 1:
                    mixing_matrix(0)
                carry(0, j)
            for i in range(GROUPS * TT):
                g, c = divmod(i, TT)
                f, b = slice(HG * g, HG * g + HG), slice(HEADS + HG * g, HEADS + HG * g + HG)
                gi = slice(GI * g, GI * g + GI)
                more = g + 1 < GROUPS and c < TT - 1
                if more:
                    weighted_x(g + 1, c)
                if i + 1 < GROUPS * TT:
                    mixing_matrix(i + 1)
                y0, y1, y2 = ty[:, 0], ty[:, 1], ty[:, 2]
                n.done(tt(h3(y0), h3(xs[:, c, gi]), bc(d_row[:, f]), ALU.mult))
                dve.wait_ge(s.yd_ps, i + 1)
                if c >= 1:
                    n.done(tt(h3(y1), h3(ps[:, 6, 0:GI]), bc(e_cs[:, c, f]), ALU.mult))
                if c < TT - 1:
                    n.done(tt(h3(y2), h3(ps[:, 7, 0:GI]), bc(e_cs[:, c, b]), ALU.mult))
                n.wait()
                for y in ([y1] if c >= 1 else []) + ([y2] if c < TT - 1 else []):
                    n.link(tt(y0, y0, y, ALU.add))
                tt(y0, y0, ps[:, 5, 0:GI], ALU.add).then_inc(s.y_read, 1)
                dve.wait_ge(s.y_read, i + 1)
                dve.wait_ge(s.z_silu, g * TT + c + 1)
                n.link(tt(ty[:, 3], y0, zg[g % 2][:, c], ALU.mult))
                dve.tensor_tensor_reduce(out=y0, in0=ty[:, 3], in1=ty[:, 3], scale=1.0, scalar=0.0, op0=ALU.mult, op1=ALU.add,
                                         accum_out=rms[:, i % 2, 0:1]).then_inc(s.gate_ready, 1)
                if more:
                    carry(g + 1, c)
                dve.wait_ge(s.rms_sqrt, i + 1)
                n.link(dve.reciprocal(rms[:, i % 2, 2:3], rms[:, i % 2, 1:2]))
                if i >= 1:
                    dve.wait_ge(s.yt_ps, i)
                ts(ty[:, 4], ty[:, 3], rms[:, i % 2, 2:3], None, ALU.mult).then_inc(s.yn_ready, 1)
                dve.wait_ge(s.gate_ready, i + 1)
            dve.wait_ge(s.sg_loaded, 64)
            for hf in range(2):
                cs = slice(512 * hf, 512 * hf + 512)
                for c in range(TT):
                    o = mix[:, c, cs]
                    dve.wait_ge(s.mix_ps, TT * (3 * hf + 1) + c + 1)
                    dve.wait_ge(s.mix_sig, TT * hf + c + 1)
                    tt(o, ps[:, m_bank[(3 * hf + 1) % 2][c], :], sg_u[:, c, :], ALU.mult).then_inc(s.mix_read, 1)
                    dve.wait_ge(s.mix_read, 2 * TT * hf + c + 1)
                    tt(o, o, sg[:, hf, 1, c, :], ALU.mult).then_inc(s.glu_done, 1)
                for c in range(TT):
                    o = mix[:, c, cs]
                    dve.wait_ge(s.mix_ps, TT * (3 * hf + 2) + c + 1)
                    if hf or c:
                        dve.wait_ge(s.mix_ready, TT * hf + c)
                    tt(tmix, ps[:, m_bank[(3 * hf + 2) % 2][c], :], sg[:, hf, 0, c, :], ALU.mult).then_inc(s.mix_read, 1)
                    dve.wait_ge(s.mix_read, TT * (2 * hf + 1) + c + 1)
                    dve.wait_ge(s.glu_done, TT * hf + c + 1)
                    tt(o, o, tmix, ALU.add).then_inc(s.mix_ready, 1)

            def moments(x, c, ready):
                for j in range(2):
                    n.done(dve.bn_stats(stats[:, j, :], x[:, 512 * j:512 * j + 512]))
                n.wait()
                dve.bn_aggr(mv[:, c, 0:2], stats).then_inc(ready, 1)

            def centred(x, out, c):
                n.link(stt(out, x, mv[:, c, 0:1], lnrow[:, 0, :], ALU.subtract, ALU.mult))

            def normed(out, c):
                return stt(out, out, mv[:, c, 3:4], lnrow[:, 1, :], ALU.mult, ALU.add)

            dve.wait_ge(s.xres_loaded, 16)
            dve.wait_ge(s.ln_loaded, 32)
            for c in range(TT):
                for j in range(2):
                    dve.wait_ge(s.wo_ps, 2 * c + j + 1)
                    r = stt(x_res[:, c, 512 * j:512 * j + 512], x_res[:, c, 512 * j:512 * j + 512], ALPHA,
                            ps[:, o_bank[c % 2][j], :], ALU.mult, ALU.add)
                    r.then_inc(s.wo_read, 1)
                dve.wait_ge(s.wo_read, 2 * c + 2)
                moments(x_res[:, c, :], c, s.var_ready)
                dve.wait_ge(s.var_ready, c + 1)
                centred(x_res[:, c, :], h[:, c, :], c)
                dve.wait_ge(s.std_ready, c + 1)
                n.link(dve.reciprocal(mv[:, c, 3:4], mv[:, c, 2:3]))
                normed(h[:, c, :], c).then_inc(s.h_ready, 1)
            dve.wait_ge(s.logit_ps, TT)
            lg = ps[:, 5, 0:TT * EXPERTS].rearrange("p (c e) -> p c e", c=TT)
            n.done(dve.tensor_copy(logit, lg))
            n.link(dve.tensor_reduce(sm[:, 0, :], lg, AX.X, ALU.max))
            ts(sm[:, 1, :], sm[:, 0, :], -1.0, None, ALU.mult).then_inc(s.max_ready, 1)
            dve.wait_ge(s.rexp_done, 1)
            n.link(dve.reciprocal(sm[:, 3, :], sm[:, 2, :]))
            tt(aff, ex_t, last(sm[:, 3, :], EXPERTS), ALU.mult).then_inc(s.aff_ready, 1)
            dve.wait_ge(s.affT_copied, 1)
            for r in range(CAP // 8):
                src = affT if r == 0 else work
                n.link(dve.max(top8[:, r, :], src))
                n.link(dve.match_replace(work, top8[:, r, :], src, -1.0))
            n.link(tt(affT, affT, work, ALU.not_equal))
            n.link(dve.tensor_tensor_scan(work, affT, affT, 0.0, ALU.add, ALU.bypass))
            tt(cum, work, affT, ALU.mult).then_inc(s.slotT_ready, 1)
            dve.wait_ge(s.slots_ready, 1)
            dve.wait_ge(s.acc_init, TT)
            with dve.Fori(0, EXPERTS // 4) as it:
                for u in range(2):
                    pair = 2 * it + u
                    e0 = bass.ds(4 * it + 2 * u, 2)
                    numbers = slot_no.unsqueeze(1).unsqueeze(1).to_broadcast([P, TT, 2, CAP])
                    tt(sel, numbers, last(slotv[:, :, e0], CAP), ALU.is_equal).then_inc(s.sel_built, 1)
                    dve.wait_ge(s.sel_built, pair + 1)
                    tt(selg, sel, last(aff[:, :, e0], CAP), ALU.mult).then_inc(s.sel_ready, 1)
                    for c in range(NCH):
                        i = NCH * u + c
                        dve.wait_ge(s.silu_pair, 2 * NCH * it + i + 1)
                        if i >= 2:
                            dve.wait_ge(s.hidT_ps, 2 * NCH * it + i - 1)
                        tt(hid[:, i % 2, :], s_h1[:, i % 2, :], ps[:, i % 2, 256:512], ALU.mult).then_inc(s.hid_ready, 1)
                    for k in range(2 * TT):
                        c, j = divmod(k, 2)
                        o = acc[:, c, 512 * j:512 * j + 512]
                        dve.wait_ge(s.sc_ps, 2 * TT * pair + k + 1)
                        tt(o, o, ps[:, 5 + k % 2, :], ALU.add).then_inc(s.acc_added, 1)
                    dve.wait_ge(s.acc_added, 2 * TT * pair + 2 * TT)
            dve.wait_ge(s.ln_loaded, 64)
            for c in range(TT):
                if c:
                    dve.wait_ge(s.ln2_var, c)
                moments(acc[:, c, :], c, s.ln2_var)
            dve.wait_ge(s.ln2_var, TT)
            for c in range(TT):
                centred(acc[:, c, :], acc[:, c, :], c)
                if c == 0:
                    dve.wait_ge(s.ln2_std, 1)
                    n.link(dve.reciprocal(mv[:, :, 3:4], mv[:, :, 2:3]))
                normed(acc[:, c, :], c).then_inc(s.ln2_ready, 1)


NAMES = ["x", "w_in", "conv_w", "conv_b", "ssd_a_log_f", "ssd_a_log_b", "ssd_dt_bias_f", "ssd_dt_bias_b", "ssd_d",
         "ssd_norm_g", "w_out_ssd", "s5_a_re_f", "s5_a_im_f", "s5_log_step_f", "s5_a_re_b", "s5_a_im_b", "s5_log_step_b",
         "s5_b_re", "s5_b_im", "s5_c_re", "s5_c_im", "s5_d", "w_glu_a", "w_glu_b", "w_o", "ln1_g", "ln1_b", "w_router",
         "w_e1", "w_e3", "w_e2", "ln2_g", "ln2_b"]


def kernel(**inputs):
    import concourse.bacc as bacc
    from concourse.bass_utils import run_bass_kernel_spmd

    nc = bacc.Bacc("TRN2", target_bir_lowering=False, num_devices=1)
    arrays = {f"in_{n}": np.ascontiguousarray(inputs[n]) for n in NAMES}
    aps = {n: nc.dram_tensor(f"in_{n}", arrays[f"in_{n}"].shape, F32, kind="ExternalInput").ap() for n in NAMES}
    out = nc.dram_tensor("out", (1, SEQ, D_MODEL), F32, kind="ExternalOutput").ap()
    encoder(nc, aps, out)
    return run_bass_kernel_spmd(nc, [arrays], core_ids=[0]).results[0]["out"]
```
